# Optimizing a Trainium2 kernel written in Bass

```python
import math, functools
import jax, jax.numpy as jnp
from jax import lax
import numpy as np

D_MODEL = 1024
BATCH = 1
SEQ = 512
DEPTH = 1
DEC_BATCH = 1
DEC_SEQ = 256
PAST_LEN = 128

D_MIX = D_MODEL
D_ATT = D_MIX // 2
D_CONV = D_MIX - D_ATT
ATT_HEAD_DIM = 64
N_ATT_HEADS = D_ATT // (2 * ATT_HEAD_DIM)
N_MAPS = 2 * N_ATT_HEADS
V_HEAD_DIM = 2 * ATT_HEAD_DIM
CONV_WIDTH = 3
D_IN = 3 * D_ATT + 3 * D_CONV
Q_BLOCK = 128
NUM_BUCKETS = 32
MAX_DISTANCE = 128
N_GROUPS = 4
EXPERTS_PER_GROUP = 4
N_EXPERTS = N_GROUPS * EXPERTS_PER_GROUP
TOP_K_IN_GROUP = 2
D_EXPERT = 256
PLE_DIM = 256
EPS = 1e-6

kernel_name = "hymba_diffattn_shortconv_hmoe_encoder"

def rmsnorm(x, g):
    xf = x.astype(jnp.float32)
    y = xf * lax.rsqrt(jnp.mean(xf * xf, axis=-1, keepdims=True) + EPS)
    return (y * g.astype(jnp.float32)).astype(x.dtype)

def t5_bucket(rel):
    half = NUM_BUCKETS // 2
    max_exact = half // 2
    ret = (rel > 0).astype(jnp.int32) * half
    n = jnp.abs(rel)
    nf = jnp.maximum(n, 1).astype(jnp.float32)
    large = max_exact + (jnp.log(nf / max_exact) / math.log(MAX_DISTANCE / max_exact)
                         * (half - max_exact)).astype(jnp.int32)
    large = jnp.minimum(large, half - 1)
    return ret + jnp.where(n < max_exact, n, large)

def diff_attention(q, k, v, lam, rel_bias):
    B, _, S, d = q.shape
    nb = S // Q_BLOCK
    scale = 1.0 / math.sqrt(ATT_HEAD_DIM)
    q_blocks = q.reshape(B, N_MAPS, nb, Q_BLOCK, d).transpose(2, 0, 1, 3, 4)
    starts = jnp.arange(nb, dtype=jnp.int32) * Q_BLOCK
    k_pos = jnp.arange(S, dtype=jnp.int32)

    def one_block(args):
        qb, start = args
        q_pos = start + jnp.arange(Q_BLOCK, dtype=jnp.int32)
        bucket = t5_bucket(k_pos[None, :] - q_pos[:, None])
        bias = rel_bias[bucket].astype(jnp.float32).transpose(2, 0, 1)
        s = jnp.einsum('bhqd,bhkd->bhqk', qb, k).astype(jnp.float32) * scale + bias[None]
        p = jax.nn.softmax(s, axis=-1).reshape(B, N_ATT_HEADS, 2, Q_BLOCK, S)
        a = (p[:, :, 0] - lam * p[:, :, 1]).astype(v.dtype)
        return jnp.einsum('bhqk,bhkv->bhqv', a, v)

    o = lax.map(one_block, (q_blocks, starts))
    return o.transpose(1, 0, 3, 2, 4).reshape(B, S, N_ATT_HEADS, V_HEAD_DIM)

def short_conv3(h, w):
    hp = jnp.pad(h, ((0, 0), (1, 1), (0, 0)))
    return w[0] * hp[:, :-2] + w[1] * hp[:, 1:-1] + w[2] * hp[:, 2:]

def hier_moe(h, w_group, b_group, w_erouter, b_erouter, w_gate_up, w_down):
    B, S, D = h.shape
    t = h.reshape(B * S, D)
    g_logits = (t @ w_group + b_group).astype(jnp.float32)
    p_group = jax.nn.softmax(g_logits, axis=-1)
    g_idx = jnp.argmax(p_group, axis=-1)
    g_w = jnp.max(p_group, axis=-1)
    e_logits = (t @ w_erouter + b_erouter).astype(jnp.float32).reshape(-1, N_GROUPS, EXPERTS_PER_GROUP)
    e_sel = jnp.take_along_axis(e_logits, g_idx[:, None, None], axis=1)[:, 0]
    p_exp = jax.nn.softmax(e_sel, axis=-1)
    top_v, top_i = lax.top_k(p_exp, TOP_K_IN_GROUP)
    top_v = top_v / jnp.sum(top_v, axis=-1, keepdims=True)
    expert_id = g_idx[:, None] * EXPERTS_PER_GROUP + top_i
    combine = jnp.sum(jax.nn.one_hot(expert_id, N_EXPERTS, dtype=jnp.float32)
                      * (g_w[:, None] * top_v)[..., None], axis=1).astype(h.dtype)
    out = jnp.zeros_like(t)
    for e in range(N_EXPERTS):
        gu = t @ w_gate_up[e]
        y = (jax.nn.silu(gu[:, :D_EXPERT]) * gu[:, D_EXPERT:]) @ w_down[e]
        out = out + combine[:, e:e + 1] * y
    return out.reshape(B, S, D)

def encode(x, p, norm_mix, w_in, q_norm, k_norm, lambda_q1, lambda_k1, lambda_q2, lambda_k2,
           attn_sub_norm, conv_w, w_out, rel_bias, norm_ffn, w_group, b_group, w_erouter, b_erouter,
           w_gate_up, w_down, w_ple_proj, w_ple_gate, ple_norm):
    B, S, _ = x.shape
    for i in range(DEPTH):
        h = rmsnorm(x, norm_mix[i])
        z = h @ w_in[i]
        q, k, v, b_g, c_g, xc = jnp.split(
            z, [D_ATT, 2 * D_ATT, 3 * D_ATT, 3 * D_ATT + D_CONV, 3 * D_ATT + 2 * D_CONV], axis=-1)
        q = rmsnorm(q.reshape(B, S, N_MAPS, ATT_HEAD_DIM), q_norm[i]).transpose(0, 2, 1, 3)
        k = rmsnorm(k.reshape(B, S, N_MAPS, ATT_HEAD_DIM), k_norm[i]).transpose(0, 2, 1, 3)
        v = v.reshape(B, S, N_ATT_HEADS, V_HEAD_DIM).transpose(0, 2, 1, 3)
        lambda_init = 0.8 - 0.6 * math.exp(-0.3 * i)
        lam = (jnp.exp(jnp.sum(lambda_q1[i].astype(jnp.float32) * lambda_k1[i].astype(jnp.float32)))
               - jnp.exp(jnp.sum(lambda_q2[i].astype(jnp.float32) * lambda_k2[i].astype(jnp.float32)))
               + lambda_init)
        o_att = diff_attention(q, k, v, lam, rel_bias)
        o_att = (rmsnorm(o_att, attn_sub_norm[i]) * (1.0 - lambda_init)).reshape(B, S, D_ATT)
        o_conv = b_g * short_conv3(c_g * xc, conv_w[i])
        x = x + jnp.concatenate([o_att, o_conv], axis=-1) @ w_out[i]
        h = rmsnorm(x, norm_ffn[i])
        x = x + hier_moe(h, w_group[i], b_group[i], w_erouter[i], b_erouter[i], w_gate_up[i], w_down[i])
        e = rmsnorm(p[i] @ w_ple_proj[i], ple_norm[i])
        x = x + jax.nn.sigmoid(x @ w_ple_gate[i]) * e
    return x

def setup_inputs(seed: int = 0) -> dict:
    key = jax.random.key(seed)
    ks = jax.random.split(key, 26)
    f32 = jnp.float32
    nrm = lambda k, shape, s: jax.random.normal(k, shape, f32) * s
    gain = lambda k, shape: 1.0 + 0.02 * jax.random.normal(k, shape, f32)
    return {
        "x_prompt": nrm(ks[0], (BATCH, SEQ, D_MODEL), 1.0),
        "x_sample": nrm(ks[1], (DEC_BATCH, DEC_SEQ, D_MODEL), 1.0),
        "p_prompt": nrm(ks[2], (DEPTH, BATCH, SEQ, PLE_DIM), 1.0),
        "p_sample": nrm(ks[3], (DEPTH, DEC_BATCH, DEC_SEQ, PLE_DIM), 1.0),
        "norm_mix": gain(ks[4], (DEPTH, D_MODEL)),
        "w_in": nrm(ks[5], (DEPTH, D_MODEL, D_IN), D_MODEL ** -0.5),
        "q_norm": gain(ks[6], (DEPTH, ATT_HEAD_DIM)),
        "k_norm": gain(ks[7], (DEPTH, ATT_HEAD_DIM)),
        "lambda_q1": nrm(ks[8], (DEPTH, ATT_HEAD_DIM), 0.1),
        "lambda_k1": nrm(ks[9], (DEPTH, ATT_HEAD_DIM), 0.1),
        "lambda_q2": nrm(ks[10], (DEPTH, ATT_HEAD_DIM), 0.1),
        "lambda_k2": nrm(ks[11], (DEPTH, ATT_HEAD_DIM), 0.1),
        "attn_sub_norm": gain(ks[12], (DEPTH, V_HEAD_DIM)),
        "conv_w": nrm(ks[13], (DEPTH, CONV_WIDTH, D_CONV), CONV_WIDTH ** -0.5),
        "w_out": nrm(ks[14], (DEPTH, D_MIX, D_MODEL), D_MIX ** -0.5),
        "rel_bias": nrm(ks[15], (NUM_BUCKETS, N_MAPS), 0.1),
        "norm_ffn": gain(ks[16], (DEPTH, D_MODEL)),
        "w_group": nrm(ks[17], (DEPTH, D_MODEL, N_GROUPS), D_MODEL ** -0.5),
        "b_group": nrm(ks[18], (DEPTH, N_GROUPS), 0.01),
        "w_erouter": nrm(ks[19], (DEPTH, D_MODEL, N_EXPERTS), D_MODEL ** -0.5),
        "b_erouter": nrm(ks[20], (DEPTH, N_EXPERTS), 0.01),
        "w_gate_up": nrm(ks[21], (DEPTH, N_EXPERTS, D_MODEL, 2 * D_EXPERT), D_MODEL ** -0.5),
        "w_down": nrm(ks[22], (DEPTH, N_EXPERTS, D_EXPERT, D_MODEL), D_EXPERT ** -0.5),
        "w_ple_proj": nrm(ks[23], (DEPTH, PLE_DIM, D_MODEL), PLE_DIM ** -0.5),
        "w_ple_gate": nrm(ks[24], (DEPTH, D_MODEL, D_MODEL), D_MODEL ** -0.5),
        "ple_norm": gain(ks[25], (DEPTH, D_MODEL)),
    }

def reference(x_prompt, x_sample, p_prompt, p_sample, norm_mix, w_in, q_norm, k_norm,
              lambda_q1, lambda_k1, lambda_q2, lambda_k2, attn_sub_norm, conv_w, w_out, rel_bias,
              norm_ffn, w_group, b_group, w_erouter, b_erouter, w_gate_up, w_down,
              w_ple_proj, w_ple_gate, ple_norm):
    layer = functools.partial(
        encode, norm_mix=norm_mix, w_in=w_in, q_norm=q_norm, k_norm=k_norm,
        lambda_q1=lambda_q1, lambda_k1=lambda_k1, lambda_q2=lambda_q2, lambda_k2=lambda_k2,
        attn_sub_norm=attn_sub_norm, conv_w=conv_w, w_out=w_out, rel_bias=rel_bias,
        norm_ffn=norm_ffn, w_group=w_group, b_group=b_group, w_erouter=w_erouter,
        b_erouter=b_erouter, w_gate_up=w_gate_up, w_down=w_down,
        w_ple_proj=w_ple_proj, w_ple_gate=w_ple_gate, ple_norm=ple_norm)
    y_prompt = layer(x_prompt, p_prompt)
    y_sample = layer(x_sample, p_sample)
    return (y_prompt, y_sample)


_drawn_inputs = setup_inputs


def setup_inputs(seed=0):
    import zlib

    import numpy as np

    out = dict(_drawn_inputs(seed))
    spreads = {}
    factors = {'q_norm': 3.594,
     'k_norm': 2.901,
     'lambda_k1': 8.0,
     'lambda_q2': 8.0,
     'attn_sub_norm': 4.706,
     'norm_ffn': 2.847,
     'b_group': 6.245,
     'b_erouter': 5.25,
     'ple_norm': 7.369}
    for name, (base, spread) in spreads.items():
        noise = np.random.default_rng([zlib.crc32(name.encode()), seed]).standard_normal(out[name].shape)
        drawn = base * np.exp(spread * noise) if base else spread * noise
        out[name] = __import__('jax').numpy.asarray(drawn.astype(out[name].dtype))
    for name, factor in factors.items():
        out[name] = (out[name] * factor).astype(out[name].dtype)
    return out
```

```python
from contextlib import ExitStack

import numpy as np

import concourse.bass as bass
from concourse import mybir

F32 = mybir.dt.float32
F32R = mybir.dt.float32r
I32 = mybir.dt.int32
U32 = mybir.dt.uint32
ALU = mybir.AluOpType
ACT = mybir.ActivationFunctionType
AX_X = mybir.AxisListType.X

P = 128
D = 1024
KD = D // P
SEQS = (512, 256)
TOK = sum(SEQS)
TILES = TOK // P
PROMPT_TILES = SEQS[0] // P
D_ATT = 512
HEADS = 4
MAPS = 2 * HEADS
HD = 64
VD = 128
BUCKETS = 32
MAX_DISTANCE = 128
G = 4
EPG = 4
E = G * EPG
DE = 256
PLE = 256
EPS = 1e-6
LAMBDA_INIT = 0.2
N = 512
ROUTES = G + E

PAIRS = 2 * TOK
OVER_TILES = PAIRS // (P + 1)
MOE_TILES = E + OVER_TILES

CONV_B, X_B, GATE_B, Q_B, K_B, V_B = range(6)
IN_UNITS, OUT_UNITS, PLE_UNITS, MOE_UNITS, FIN_UNITS = 24, 8, 2, 6, 8
OUT0 = IN_UNITS
PLE0 = OUT0 + OUT_UNITS
MOE0 = PLE0 + PLE_UNITS
WS = 8
RS = 6

GW = 896
REL = 1024

C_ID, C_U, C_ONE, C_J, C_DESC, C_E128, C_K15, C_THR, C_T = 0, 128, 256, 384, 512, 516, 532, 548, 554
C_N = C_T + E


def constants():
    c = np.zeros((P, C_N), np.float32)
    c[:, C_ID:C_ID + P] = np.eye(P)
    c[:, C_U:C_U + P] = np.triu(np.ones((P, P)), 1)
    c[:, C_ONE:C_ONE + P] = 1
    c[:, C_J:C_J + P] = np.eye(P)[::-1]
    c[:, C_DESC:C_DESC + 4] = [4, 3, 2, 1]
    c[:, C_E128:C_E128 + E] = P * np.arange(E)
    c[:, C_K15:C_K15 + E] = P * (E - 1 - np.arange(E))
    c[:, C_THR:C_THR + 6] = P * np.arange(1, 7)
    c[:, C_T:C_T + E] = np.arange(E)
    rel = np.arange(REL) - REL // 2
    n = np.abs(rel)
    starts = [1, 2, 3, 4, 5, 6, 7, 8, 12, 16, 23, 32, 46, 64, 91]
    bucket = sum((n >= s).astype(int) for s in starts) + np.where(rel > 0, BUCKETS // 2, 0)
    hot = (np.arange(BUCKETS)[:, None] == bucket[None, :]).astype(np.float32)
    return c, hot


def build(nc, x, pT, w_in, w_out, w_ple, w_moe, w_gate, w_route, gains, cols, rows, rel_bias,
          consts, hot, y_prompt, y_sample):
    bias_dram = nc.dram_tensor("bias_table", (MAPS, REL), F32, kind="Internal").ap()
    slots_dram = nc.dram_tensor("slot_rows", (MOE_TILES * P, D), F32, kind="Internal").ap()

    ctx = ExitStack()
    with ctx:
        base = 16512
        sizes = dict(W=WS * 8192, RAW=RS * 4096, A=49152, R1=12288, R2=12288, R3=12288, R4=12288,
                     TMP=8192, X=7168, S=9568)
        at, o = {}, base
        for k, v in sizes.items():
            at[k] = o
            o += v

        def sb(name, shape, dt, region, off=0):
            return nc.alloc_sbuf_tensor_at(name, shape, dt, offset=at[region] + off)

        small = [0]

        def sm(name, n, dt=F32):
            t = sb(name, [P, n], dt, "S", small[0])
            small[0] += (4 * n + 31) // 32 * 32
            assert small[0] <= sizes["S"], small[0]
            return t

        W = sb("w_split", [P, WS, 2, 2, N], F32R, "W")
        RAW = sb("w_raw", [P, RS, 2, N], F32, "RAW")
        hT = sb("h_T", [P, 2, KD, TOK], F32R, "A")
        xt = [sb(f"x_tile{i}", [P, D], F32, "TMP", 4096 * i) for i in range(2)]
        tok_tmp = [sb(f"tok_tmp{i}", [P, N], F32, "TMP", 2048 * i) for i in range(2)]
        sq_tmp = sb("sq_tmp", [P, N], F32, "TMP", 4096)
        u_tok = sb("u_tok", [P, TILES, N], F32, "R1")
        uT = sb("u_T", [P, 4, TOK], F32, "R2")
        convT = sb("conv_T", [P, 4, TOK], F32, "R1")
        qT = sb("q_T", [P, HEADS, TOK], F32, "R3")
        kT = sb("k_T", [P, HEADS, TOK], F32, "R2")
        v = sb("v_tok", [P, TILES, N], F32, "R4")
        zeros = sb("zeros", [P, 768], F32, "X")
        junk = sb("junk", [P, D], F32, "X", 3072)
        hot_sb = sb("hot_sb", [BUCKETS, REL], F32, "R3")
        bias_sb = sb("bias_sb", [MAPS, REL], F32, "R3", 4096)
        o_tok = sb("o_tok", [P, TILES, N], F32, "A")
        mixA = [sb(f"mix_att{i}", [P, HEADS, TOK], F32R, "A", 12288 * (1 + i)) for i in range(2)]
        toep = [sb("toep0", [P, 2, GW], F32, "A", 36864), sb("toep1", [P, 2, GW], F32, "X")]
        aT = [sb(f"a_T{i}", [P, N], F32, "A", 44032 + 2048 * i) for i in range(2)]
        ojunk = sb("o_junk", [P, VD], F32, "A", 48128)
        s_sb = [[sb(f"s{i}_{m}", [P, N], F32, "TMP", 4096 * i + 2048 * m) for m in range(2)]
                for i in range(2)]
        mixC = [sb("mix_conv0", [P, 4, TOK], F32R, "R2"), sb("mix_conv1", [P, 4, TOK], F32R, "R3")]
        x2 = [sb(f"x2_{i}", [P, D], F32, "R1" if i < 3 else "R4", 4096 * (i % 3)) for i in range(TILES)]
        h2 = [sb(f"h2_{i}", [P, D], F32, "A", 4096 * (i % 3) + (0 if i < 3 else 36864))
              for i in range(TILES)]
        xr = [sb(f"x_again{i}", [P, D], F32, "TMP", 4096 * i) for i in range(2)]
        h2T = sb("h2_T", [P, KD, P], F32, "X")
        pTs = [sb(f"p_T{i}", [P, 2, TOK], F32R, "R2", 6144 * i) for i in range(2)]
        p_raw = sb("p_raw", [P, 2, TOK], F32, "R3")
        ejunk = sb("e_junk", [P, D], F32, "R3", 6144)
        ple = [sb(f"ple{i}", [P, D], F32, "A", 12288 + 4096 * i) for i in range(TILES)]
        xg = sb("moe_x", [P, D], F32, "R2")
        xgT = [sb(f"moe_xT{i}", [P, KD, P], F32R, "R2", 4096 * (1 + i)) for i in range(2)]
        actT = [sb(f"moe_actT{i}", [P, 2, P], F32R, "R3", 1024 * i) for i in range(2)]
        sg = sb("moe_silu", [P, DE], F32, "R3", 2048)
        act_t = sb("moe_act", [P, DE], F32, "R3", 3072)
        yb = sb("moe_y", [P, 2, N], F32, "R3", 4096)
        ga = [sb("pick0_0", [P, D], F32, "A", 0), sb("pick0_1", [P, D], F32, "A", 36864)]
        gb = [sb("pick1_0", [P, D], F32, "A", 4096), sb("pick1_1", [P, D], F32, "A", 40960)]
        x3T = [[sb(f"x3T{i}_{j}", [P, KD, P], F32R, "R2" if 2 * i + j < 3 else "R3",
                   4096 * ((2 * i + j) % 3)) for j in range(2)] for i in range(2)]
        sig = sb("sig", [P, D], F32, "R3", 4096)
        outb = sb("out_tile", [P, D], F32, "R3", 8192)
        roff = [0]

        def rt(name, *shape):
            n = int(np.prod(shape))
            t = sb(name, [P, *shape], F32, "TMP", roff[0])
            roff[0] += (4 * n + 31) // 32 * 32
            assert roff[0] <= 8192
            return t

        r_lg = rt("r_lg", TILES, ROUTES)
        r_gm = rt("r_gm", TILES)
        r_ge = rt("r_ge", TILES, G)
        r_gs = rt("r_gs", TILES)
        r_oh = rt("r_oh", TILES, G)
        r_sc = rt("r_sc", TILES, G)
        r_sel = rt("r_sel", TILES, EPG)
        r_m1, r_m2 = rt("r_m1", TILES), rt("r_m2", TILES)
        r_o1, r_o2 = rt("r_o1", TILES, EPG), rt("r_o2", TILES, EPG)
        r_e2 = rt("r_e2", TILES)
        r_O = [rt(f"r_O{j}", TILES, G, EPG) for j in range(2)]
        r_M = rt("r_M", TILES + 1, E)
        r_C = rt("r_C", TILES, E)
        r_big = rt("r_big", TILES, E)
        r_slot = rt("r_slot", TILES, E)
        r_t = rt("r_t", TILES, E)
        r_cnt = rt("r_cnt", E)
        r_ov = rt("r_ov", E, 6)
        r_b = rt("r_b", E)
        r_inc = rt("r_inc", E)
        r_base = rt("r_base", E)
        r_et = rt("r_et", OVER_TILES, E)
        r_ef = rt("r_ef", OVER_TILES + 1)

        cst = sm("cst", C_N)
        gain = sb("gain_row", [P, D], F32, "S", small[0])
        pad = [sb(f"q_pad{i}", [P, 2, P], F32, "S", small[0] + 1024 * i) for i in range(2)]
        lamv = sb("lam_rows", [P, 4 * HD], F32, "R4")
        small[0] += 4096
        colv = sm("colv", 16)
        bias_row = sm("bias_row", ROUTES)
        relb = sm("relb", MAPS)
        wr = sb("w_route_sb", [P, KD, ROUTES], F32, "S", small[0])
        small[0] += 4 * KD * ROUTES
        eps = sm("eps_t", 1)
        lam = sm("lam_t", 8)
        gs = sm("gs_t", 1)
        x_ssq, x_std = sm("x_ssq", TILES), sm("x_std", TILES)
        qk_ss = sm("qk_ss", 96)
        mx, nmx, Z, rz = (sm(n, 48) for n in ("mx", "nmx", "Z", "rz"))
        ratio, o_ssq = sm("ratio", 24), sm("o_ssq", 24)
        x2_ssq = sm("x2_ssq", TILES)
        e_ssq = sm("e_ssq", TILES)
        slot_u = sm("slot_u", 2 * TILES, U32)
        wgt = sm("wgt", 2 * TILES)
        etab = sm("etab", MOE_TILES, I32)
        last_tile = sm("last_tile", 1, I32)

        bank = [ctx.enter_context(nc.psum_tensor(f"bank{i}", [P, N], F32)) for i in range(8)]

        def sem(name):
            return ctx.enter_context(nc.semaphore(name))

        c_ld = sem("consts_loaded")
        gain_ld = sem("gain_loaded")
        raw_ld = [sem(f"raw_loaded{i}") for i in range(RS)]
        hi_done, lo_done = sem("w_hi_done"), sem("w_lo_done")
        w_used = sem("w_unit_used")
        x_ld = [sem(f"x_loaded{i}") for i in range(2)]
        a_x, d_x = sem("act_x_stats"), sem("dve_x_normed")
        pe_t, t_hi = sem("pe_transposed"), sem("act_hT_hi")
        t_free = [sem(f"t_bank_free{i}") for i in range(4)]
        pe_acc = sem("pe_projected")
        acc_free = [sem(f"acc_bank_free{i}") for i in range(3)]
        dch = sem("dve_steps")
        ach = sem("act_steps")
        gch = sem("pool_steps")
        a_sq, d_ss, a_sd = sem("act_qk_square"), sem("dve_qk_sum"), sem("act_qk_std")
        a_lam = sem("act_lambda_exp")
        z_done, z_st = sem("zeros_set"), sem("slots_zeroed")
        pe_b, a_b, b_st = sem("pe_bias"), sem("act_bias"), sem("bias_stored")
        toep_ld = [sem(f"toep_loaded{i}") for i in range(2)]
        p_pad, pe_s, d_s, d_nm, a_e, d_a = (sem(n) for n in (
            "pool_q_padded", "pe_scores", "dve_scores", "dve_neg_max", "act_exp", "dve_a"))
        pe_at, a_at, pe_o, d_o, d_oss = (sem(n) for n in (
            "pe_aT", "act_aT", "pe_o", "dve_o", "dve_o_ssq"))
        a_os, d_on, pe_ot, a_mix, d_mix, a_mixc, d_mixc = (sem(n) for n in (
            "act_o_std", "dve_o_normed", "pe_oT", "act_mix_hi", "dve_mix_lo", "act_conv_hi",
            "dve_conv_lo"))
        xr_ld = [sem(f"x_again{i}") for i in range(2)]
        pe_wo, d_x2, a_x2, d_h2, pe_h2, a_h2, pe_r = (sem(n) for n in (
            "pe_out_proj", "dve_x2", "act_x2_stats", "dve_h2", "pe_h2T", "act_h2T", "pe_routes"))
        d_lg, a_g, a_e2, d_m, pe_rk, d_route = (sem(n) for n in (
            "dve_logits", "act_group_exp", "act_second_exp", "dve_masks", "pe_ranks", "dve_routed"))
        p_ld, a_p, d_p, pe_ple, a_ple, d_ple, g_ple = (sem(n) for n in (
            "p_loaded", "act_p_hi", "dve_p_lo", "pe_ple", "act_ple", "dve_ple_std", "pool_ple"))
        scat = sem("rows_scattered")
        xg_ld, pe_xt, a_xt, d_xt = (sem(n) for n in (
            "moe_x_loaded", "pe_moe_xT", "act_moe_xT_hi", "dve_moe_xT_lo"))
        pe_gu, a_si, d_act, pe_aT2, a_aT2, d_aT2, pe_y, a_y, d_y = (sem(n) for n in (
            "pe_gate_up", "act_silu", "dve_act", "pe_actT", "act_actT_hi", "dve_actT_lo",
            "pe_down", "act_y", "dve_y"))
        y_st = [sem(f"y_stored{i}") for i in range(2)]
        y_free = [sem(f"y_half_free{i}") for i in range(2)]
        pk_ld = [sem(f"picked{i}") for i in range(2)]
        d_x3, pe_x3, a_x3, d_x3t, pe_g, a_g2, d_out, o_st = (sem(n) for n in (
            "dve_x3", "pe_x3T", "act_x3_hi", "dve_x3_lo", "pe_gate", "act_sigmoid", "dve_out",
            "out_stored"))

        ident = cst[:, C_ID:C_ID + P]

        def tk(i):
            return slice(i * P, (i + 1) * P)

        def f(t):
            return t.bitcast(F32)

        def slot_free(eng, u):
            v0 = u - WS
            if v0 < 0:
                return
            if v0 < OUT0:
                b, j = divmod(v0, 4)
                if j < 3:
                    eng.wait_ge(w_used, 3 * b + j + 1)
                else:
                    eng.wait_ge(pe_acc, TILES * (b + 1))
            else:
                out_unit_used(eng, v0 - OUT0)

        def out_unit_used(eng, j):
            if j % 4 < 3:
                eng.wait_ge(w_used, 18 + 3 * (j // 4) + j % 4 + 1)
            else:
                eng.wait_ge(pe_wo, 2 * (TILES - 1) + 1 + j // 4)

        def moe_unit_used(eng, t, j):
            if j < 3:
                eng.wait_ge(w_used, t * 3 + (24 + j + 1))
            elif j == 3:
                eng.wait_ge(pe_gu, t + 1)
            else:
                eng.wait_ge(pe_y, t * 2 + (j - 3))

        def split_hi(u, t=0):
            s = u % RS
            nc.scalar.wait_ge(raw_ld[s], t * 16 + 16 * (u // RS + 1))
            nc.scalar.activation(W[:, u % WS, 0], RAW[:, s], ACT.Copy).then_inc(hi_done, 1)

        def split_lo(u, t=0, slot=None):
            s, w = u % RS, (u % WS if slot is None else slot)
            nc.vector.wait_ge(hi_done, t * 6 + (u + 1))
            nc.vector.tensor_tensor(W[:, w, 1], RAW[:, s], f(W[:, w, 0]),
                                    ALU.subtract).then_inc(lo_done, 1)

        def three(out, hi, lo, whi, wlo, first, last):
            nc.tensor.matmul(out, hi, whi, start=first, stop=False)
            nc.tensor.matmul(out, lo, whi, start=False, stop=False)
            return nc.tensor.matmul(out, hi, wlo, start=False, stop=last)

        def t_ready(eng, m):
            eng.wait_ge(t_free[m % 4], m // 4 + 1)

        TJ = {X_B: 12, GATE_B: 18, Q_B: 24, K_B: 30}
        def keys(i):
            return (0, SEQS[0]) if i < PROMPT_TILES else (SEQS[0], SEQS[1])

        ITEMS = [(h, i) for h in range(HEADS) for i in range(TILES)]
        NI = len(ITEMS)

        block = ctx.enter_context(nc.Block())

        @block.sync
        def _(sp):
            def unit(src, u):
                if u >= RS:
                    sp.wait_ge(lo_done, u - RS + 1)
                sp.dma_start(RAW[:, u % RS], src).then_inc(raw_ld[u % RS], 16)

            def x_tile(i):
                if i >= 2:
                    sp.wait_ge(pe_t, 2 * (i - 2) + 2)
                sp.dma_start(xt[i % 2][:], x[tk(i)]).then_inc(x_ld[i % 2], 16)

            sp.dma_start(gain[:], gains[0]).then_inc(gain_ld, 16)
            x_tile(0)
            x_tile(1)
            for u in range(4):
                unit(w_in[u], u)
            for i in range(2, TILES):
                x_tile(i)
            for u in range(4, OUT0 + 4):
                unit(w_in[u] if u < OUT0 else w_out[u - OUT0], u)
                if u == 8:
                    sp.wait_ge(a_b, 2)
                    sp.dma_start(bias_dram, bias_sb[:]).then_inc(b_st, 16)
            sp.wait_ge(b_st, 16)

            def toeplitz(h):
                if h == 0:
                    sp.wait_ge(pe_acc, 36)
                elif h == 1:
                    sp.wait_ge(z_st, 16)
                    sp.wait_ge(ach, 6)
                else:
                    sp.wait_ge(d_s, 2 * TILES * (h - 1))
                src = bass.AP(bias_dram.tensor, 2 * h * REL + 1,
                              [[1, P], [REL, 2], [1, GW]])
                sp.dma_start(toep[h % 2][:], src).then_inc(toep_ld[h % 2], 16)

            toeplitz(0)
            toeplitz(1)
            for u in range(OUT0 + 4, PLE0):
                unit(w_out[u - OUT0], u)
            toeplitz(2)
            toeplitz(3)
            sp.wait_ge(pe_s, 2 * NI)
            sp.dma_start(gain[:], gains[1]).then_inc(gain_ld, 16)
            sp.wait_ge(pe_at, NI)
            for i in range(TILES):
                if i >= 2:
                    sp.wait_ge(d_x2, 2 * (i - 2) + 2)
                if i == 2:
                    for u in range(PLE0, MOE0):
                        unit(w_ple[u - PLE0], u)
                sp.dma_start(xr[i % 2][:], x[tk(i)]).then_inc(xr_ld[i % 2], 16)
            for j in range(4):
                unit(w_moe[0, j], MOE0 + j)
            sp.wait_ge(pe_wo, 2 * TILES)
            sp.dma_start(p_raw[:], pT).then_inc(p_ld, 16)
            for j in range(4, MOE_UNITS):
                unit(w_moe[0, j], MOE0 + j)
            sp.wait_ge(d_h2, TILES)
            sp.dma_start(gain[:], gains[2]).then_inc(gain_ld, 16)
            sp.wait_ge(scat, 16 * 2 * TILES)
            sp.wait_ge(a_ple, 3 * TILES)
            sp.dma_start(xg[:], slots_dram[0:P]).then_inc(xg_ld, 16)
            sp.wait_ge(d_route, 1)
            last = sp.value_load(last_tile[0:1, 0:1], min_val=E - 1, max_val=MOE_TILES - 1)
            with sp.Fori(0, last) as t:
                sp.wait_ge(pe_xt, t * 2 + 2)
                sp.dma_start(xg[:], slots_dram[bass.ds((t + 1) * P, P)]).then_inc(xg_ld, 16)
                ex = sp.value_load(etab[0:1, bass.ds(t + 1, 1)], min_val=0, max_val=E - 1)
                for j in range(MOE_UNITS):
                    u = MOE0 + MOE_UNITS + j
                    sp.wait_ge(lo_done, t * 6 + (u - RS + 1))
                    sp.dma_start(RAW[:, u % RS], w_moe[bass.ds(ex, 1), j].rearrange(
                        "a p k n -> (a p) k n")).then_inc(raw_ld[u % RS], 16)
            for g in range(FIN_UNITS):
                u = MOE0 + g
                sp.wait_ge(lo_done, last * 6 + (u - RS + 7))
                sp.dma_start(RAW[:, u % RS], w_gate[g]).then_inc(raw_ld[u % RS], 16)
            for i in range(TILES):
                sp.wait_ge(d_out, i + 1)
                dst = y_prompt[tk(i)] if i < PROMPT_TILES else y_sample[tk(i - PROMPT_TILES)]
                sp.dma_start(dst, outb[:]).then_inc(o_st, 16)
            sp.wait_ge(o_st, 16 * TILES)

        @block.gpsimd
        def _(pool):
            pool.memset(zeros[:], 0.0).then_inc(z_done, 1)
            pool.wait_ge(z_done, 1)
            nz = MOE_TILES * D // 768
            pool.wait_ge(raw_ld[3], 16)
            pool.dma_start(slots_dram.rearrange("(p r) d -> p (r d)", p=P).rearrange(
                "p (n z) -> p n z", z=768), zeros[:].unsqueeze(1).broadcast_to([P, nz, 768])
            ).then_inc(z_st, 16)

            pool.wait_ge(d_x, 2 * TILES)
            for i in range(2):
                pool.memset(pad[i][HD:P, 0, :], 0.0).then_inc(gch, 1)
                pool.memset(pad[i][0:HD, 1, :], 0.0).then_inc(gch, 1)
            pool.wait_ge(gch, 4)
            t_ready(pool, TJ[Q_B] + 5)
            t_ready(pool, TJ[Q_B] + 4)
            t_ready(pool, TJ[Q_B] + 3)
            t_ready(pool, TJ[Q_B] + 2)
            for w, (h, i) in enumerate(ITEMS):
                if w >= 2:
                    pool.wait_ge(pe_s, 2 * (w - 1))
                for m in range(2):
                    r = slice(m * HD, (m + 1) * HD)
                    pool.tensor_copy(pad[w % 2][r, m, :], qT[r, h, tk(i)]).then_inc(p_pad, 1)

            pool.wait_ge(d_route, 1)
            pool.wait_ge(z_st, 16)
            for j in range(2):
                for i in range(TILES):
                    c = j * TILES + i
                    pool.indirect_dma_start(
                        slots_dram, bass.IndirectOffsetOnAxis(ap=slot_u[:, c:c + 1], axis=0),
                        h2[i][:], None).then_inc(scat, 16)

            pool.wait_ge(gain_ld, 48)
            for i in range(TILES):
                pool.wait_ge(d_ple, i + 1)
                pool.tensor_scalar(ple[i][:], ple[i][:], e_ssq[:, i:i + 1], None,
                                   ALU.mult).then_inc(g_ple, 1)
                pool.wait_ge(g_ple, 2 * i + 1)
                pool.tensor_tensor(ple[i][:], ple[i][:], gain[:], ALU.mult).then_inc(g_ple, 1)

            last = pool.value_load(last_tile[0:1, 0:1], min_val=E - 1, max_val=MOE_TILES - 1)

            def store_y(t):
                for half, done in ((0, a_y), (1, d_y)):
                    pool.wait_ge(done, t + 2)
                    pool.dma_start(slots_dram[bass.ds(t * P, P), half * N:(half + 1) * N],
                                   yb[:, half]).then_inc(y_st[half], 16)

            for half in range(2):
                pool.sem_inc(y_free[half], 1)
            with pool.Fori(0, last + 1) as t:
                store_y(t)
                for half in range(2):
                    pool.wait_ge(y_st[half], t * 16 + 16)
                    pool.sem_inc(y_free[half], 1)

            for i in range(TILES):
                if i >= 2:
                    pool.wait_ge(d_x3, i - 1)
                for j, buf in ((0, ga), (1, gb)):
                    c = j * TILES + i
                    pool.indirect_dma_start(
                        buf[i % 2][:], None, slots_dram,
                        bass.IndirectOffsetOnAxis(ap=slot_u[:, c:c + 1], axis=0)
                    ).then_inc(pk_ld[i % 2], 16)

        @block.scalar
        def _(act):
            act.dma_start(lamv[:], rows[:, 0:4 * HD]).then_inc(c_ld, 16)
            act.dma_start(cst[:], consts).then_inc(c_ld, 16)
            act.dma_start(colv[:, 0:15], cols).then_inc(c_ld, 16)
            act.dma_start(bias_row[:], rows[:, 4 * HD:4 * HD + ROUTES]).then_inc(c_ld, 16)
            act.dma_start(relb[0:BUCKETS, :], rel_bias).then_inc(c_ld, 16)
            act.dma_start(hot_sb[:], hot).then_inc(c_ld, 16)
            act.dma_start(wr[:], w_route).then_inc(c_ld, 16)

            def x_stats(i):
                act.wait_ge(x_ld[i % 2], 16 * (i // 2 + 1))
                if i == 0:
                    act.wait_ge(dch, 1)
                else:
                    act.wait_ge(ach, i)
                act.activation(junk[:], xt[i % 2][:], ACT.Square,
                               accum_out=x_ssq[:, i:i + 1]).then_inc(ach, 1)
                act.wait_ge(ach, i + 1)
                act.activation(x_std[:, i:i + 1], x_ssq[:, i:i + 1], ACT.Sqrt, bias=eps[:],
                               scale=1.0 / D).then_inc(a_x, 1)

            def hT_hi(i):
                for half in range(2):
                    m = 2 * i + half
                    act.wait_ge(pe_t, m + 1)
                    act.activation(hT[:, 0, 4 * half:4 * half + 4, tk(i)],
                                   bank[3 + m % 4][:].rearrange("p (k t) -> p k t", k=4),
                                   ACT.Copy).then_inc(t_hi, 1)

            x_stats(0)
            x_stats(1)
            hT_hi(0)
            split_hi(0)
            split_hi(1)
            x_stats(2)
            hT_hi(1)
            split_hi(2)
            split_hi(3)

            def next_unit(b, i):
                u = 4 * (b + 1) + i
                if i < 4:
                    slot_free(act, u)
                    split_hi(u)

            for b in range(6):
                for i in range(TILES):
                    n = TILES * b + i
                    if b == CONV_B:
                        if i + 3 < TILES:
                            x_stats(i + 3)
                        if i + 2 < TILES:
                            hT_hi(i + 2)
                        act.wait_ge(pe_acc, n + 1)
                        act.activation(u_tok[:, i], bank[n % 3][:], ACT.Copy).then_inc(acc_free[n % 3], 1)
                    elif b == X_B:
                        m = TJ[b] + i
                        act.wait_ge(pe_t, m + 1)
                        act.activation(uT[:, :, tk(i)], bank[3 + m % 4][:].rearrange(
                            "p (k t) -> p k t", k=4), ACT.Copy).then_inc(t_free[m % 4], 1)
                    elif b == GATE_B:
                        act.wait_ge(pe_acc, n + 1)
                        if i >= 2:
                            act.wait_ge(pe_t, TJ[b] + i - 1)
                        act.activation(tok_tmp[i % 2][:], bank[n % 3][:],
                                       ACT.Copy).then_inc(acc_free[n % 3], 1)
                    elif b in (Q_B, K_B):
                        r = n - TILES * Q_B
                        act.wait_ge(pe_acc, n + 1)
                        if r >= 1:
                            act.wait_ge(d_ss, r)
                        act.activation(sq_tmp[:], bank[n % 3][:], ACT.Square).then_inc(a_sq, 1)
                        act.wait_ge(d_ss, r + 1)
                        act.activation(qk_ss[:, 8 * r:8 * r + 8], qk_ss[:, 8 * r:8 * r + 8], ACT.Sqrt,
                                       bias=eps[:], scale=1.0 / HD).then_inc(a_sd, 1)
                    else:
                        act.wait_ge(pe_acc, n + 1)
                        act.activation(v[:, i], bank[n % 3][:], ACT.Copy).then_inc(acc_free[n % 3], 1)
                    next_unit(b, i)
                if b == CONV_B:
                    for half in range(2):
                        act.wait_ge(pe_b, half + 1)
                        act.activation(bias_sb[:, half * N:(half + 1) * N], bank[7][0:MAPS],
                                       ACT.Copy).then_inc(a_b, 1)
                    act.activation(lam[:, 0:2], lam[:, 0:2], ACT.Exp).then_inc(a_lam, 1)

            def evac_aT(w):
                nk = keys(ITEMS[w][1])[1]
                act.wait_ge(pe_at, w + 1)
                if w >= 2:
                    act.wait_ge(pe_o, w - 1)
                act.activation(aT[w % 2][:, 0:nk], bank[4 + w % 2][:, 0:nk], ACT.Copy).then_inc(a_at, 1)

            for w in range(NI + 2):
                if w >= 2:
                    evac_aT(w - 2)
                if w < NI:
                    nk = keys(ITEMS[w][1])[1]
                    act.wait_ge(d_nm, w + 1)
                    for m in range(2):
                        s = s_sb[w % 2][m][:, 0:nk]
                        act.activation(s, s, ACT.Exp, bias=nmx[:, 2 * w + m:2 * w + m + 1],
                                       accum_out=Z[:, 2 * w + m:2 * w + m + 1]).then_inc(a_e, 1)
                if w < 4:
                    slot_free(act, OUT0 + 4 + w)
                    split_hi(OUT0 + 4 + w)

            act.wait_ge(d_oss, NI)
            act.activation(o_ssq[:], o_ssq[:], ACT.Sqrt, bias=eps[:], scale=1.0 / VD).then_inc(a_os, 1)
            for i in range(TILES):
                act.wait_ge(pe_ot, i + 1)
                act.activation(mixA[0][:, :, tk(i)], bank[4 + i % 2][:].rearrange(
                    "p (k t) -> p k t", k=4), ACT.Copy, scale=gs[:]).then_inc(a_mix, 1)
                act.activation(mixC[0][:, :, tk(i)], convT[:, :, tk(i)], ACT.Copy).then_inc(a_mixc, 1)

            for i in range(TILES):
                if True:
                    act.wait_ge(d_x2, 2 * i + 2)
                    act.activation(h2[i][:], x2[i][:], ACT.Square,
                                   accum_out=x2_ssq[:, i:i + 1]).then_inc(a_x2, 1)
                    act.wait_ge(a_x2, 2 * i + 1)
                    act.activation(x2_ssq[:, i:i + 1], x2_ssq[:, i:i + 1], ACT.Sqrt, bias=eps[:],
                                   scale=1.0 / D).then_inc(a_x2, 1)
                    for half in range(2):
                        act.wait_ge(pe_h2, 2 * i + half + 1)
                        if half == 0 and i >= 1:
                            act.wait_ge(pe_r, i)
                        act.activation(h2T[:, 4 * half:4 * half + 4], bank[6 + half][:].rearrange(
                            "p (k t) -> p k t", k=4), ACT.Copy).then_inc(a_h2, 1)
                if i == TILES - 1:
                    act.wait_ge(pe_wo, 2 * TILES)
                    for u in range(PLE0, MOE0):
                        slot_free(act, u)
                        split_hi(u)
            act.wait_ge(p_ld, 16)
            act.activation(pTs[0][:], p_raw[:], ACT.Copy).then_inc(a_p, 1)

            act.wait_ge(d_lg, 1)
            act.activation(r_ge[:], r_ge[:], ACT.Exp).then_inc(a_g, 1)
            act.wait_ge(d_lg, 2)
            act.activation(r_e2[:], r_e2[:], ACT.Exp).then_inc(a_e2, 1)

            for i in range(TILES):
                for half in range(2):
                    act.wait_ge(pe_ple, 2 * i + half + 1)
                    act.activation(ple[i][:, half * N:(half + 1) * N], bank[2 * (i % 2) + half][:],
                                   ACT.Copy).then_inc(a_ple, 1)
                act.wait_ge(a_ple, 3 * i + 2)
                act.activation(ejunk[:], ple[i][:], ACT.Square,
                               accum_out=e_ssq[:, i:i + 1]).then_inc(a_ple, 1)
                act.wait_ge(a_ple, 3 * i + 3)
                act.activation(e_ssq[:, i:i + 1], e_ssq[:, i:i + 1], ACT.Sqrt, bias=eps[:],
                               scale=1.0 / D).then_inc(ach, 1)
                slot_free(act, MOE0 + i)
                split_hi(MOE0 + i)

            act.wait_ge(d_route, 1)
            last = act.value_load(last_tile[0:1, 0:1], min_val=E - 1, max_val=MOE_TILES - 1)

            def xT_hi(half, t=None):
                c = half + 1 if t is None else t * 2 + (3 + half)
                act.wait_ge(pe_xt, c)
                act.activation(xgT[0][:, 4 * half:4 * half + 4], bank[1 + half][:].rearrange(
                    "p (k t) -> p k t", k=4), ACT.Copy).then_inc(a_xt, 1)

            def silu(t):
                act.wait_ge(pe_gu, t + 1)
                act.wait_ge(d_act, t + 1)
                act.activation(sg[:], bank[0][:, 0:DE], ACT.Silu).then_inc(a_si, 1)

            def actT_hi(t):
                act.wait_ge(pe_aT2, t + 1)
                act.activation(actT[0][:], bank[3][:, 0:DE].rearrange("p (k t) -> p k t", k=2),
                               ACT.Copy).then_inc(a_aT2, 1)

            def y_left(t):
                act.wait_ge(pe_y, t * 2 + 1)
                act.wait_ge(y_free[0], t + 1)
                act.activation(yb[:, 0], bank[4][:], ACT.Copy).then_inc(a_y, 1)

            def moe_hi(j, t):
                moe_unit_used(act, t, j)
                s = (MOE0 + j) % RS
                act.wait_ge(raw_ld[s], t * 16 + 16 * ((MOE0 + 6 + j) // RS + 1))
                act.activation(W[:, (MOE0 + j) % WS, 0], RAW[:, s], ACT.Copy).then_inc(hi_done, 1)

            xT_hi(0)
            xT_hi(1)
            act.sem_inc(a_y, 1)
            with act.Fori(0, last) as t:
                for j in range(3):
                    moe_hi(j, t)
                silu(t)
                xT_hi(0, t)
                actT_hi(t)
                xT_hi(1, t)
                for j in range(3, 5):
                    moe_hi(j, t)
                y_left(t)
                moe_hi(5, t)
            silu(last)
            actT_hi(last)
            y_left(last)

            def gate_hi(g):
                if g < 2:
                    act.wait_ge(pe_ple, 2 * TILES)
                else:
                    moe_unit_used(act, last, g - 2)
                u = MOE0 + g
                act.wait_ge(raw_ld[u % RS], last * 16 + 16 * (u // RS + 2))
                act.activation(W[:, g % WS, 0], RAW[:, u % RS], ACT.Copy).then_inc(hi_done, 1)

            for g in range(FIN_UNITS):
                gate_hi(g)

            def x3T_hi(i):
                for half in range(2):
                    act.wait_ge(pe_x3, 2 * i + half + 1)
                    act.activation(x3T[i % 2][0][:, 4 * half:4 * half + 4], bank[6 + half][:].rearrange(
                        "p (k t) -> p k t", k=4), ACT.Copy).then_inc(a_x3, 1)

            x3T_hi(0)
            for i in range(TILES):
                if i + 1 < TILES:
                    x3T_hi(i + 1)
                for half in range(2):
                    act.wait_ge(pe_g, 2 * i + half + 1)
                    if half == 0 and i >= 1:
                        act.wait_ge(d_out, i)
                    act.activation(sig[:, half * N:(half + 1) * N], bank[2 * (i % 2) + half][:],
                                   ACT.Sigmoid).then_inc(a_g2, 1)

        @block.vector
        def _(dve):
            steps = [0]

            def link(ins):
                steps[0] += 1
                ins.then_inc(dch, 1)
                dve.wait_ge(dch, steps[0])

            link(dve.memset(eps[:], EPS))
            dve.wait_ge(c_ld, 16 * 7)
            for j in range(2):
                ins = dve.tensor_tensor_reduce(lamv[:, 2 * j * HD:(2 * j + 1) * HD],
                                               lamv[:, 2 * j * HD:(2 * j + 1) * HD],
                                               lamv[:, (2 * j + 1) * HD:(2 * j + 2) * HD], 1.0, 0.0,
                                               ALU.mult, ALU.add, lam[:, j:j + 1])
                link(ins)
            link(dve.tensor_scalar(gs[:], colv[:, 2:3], 1.0 - LAMBDA_INIT, None, ALU.mult))

            def x_norm(i):
                dve.wait_ge(a_x, i + 1)
                if i == 0:
                    dve.wait_ge(gain_ld, 16)
                dve.reciprocal(x_std[:, i:i + 1], x_std[:, i:i + 1]).then_inc(d_x, 1)
                dve.wait_ge(d_x, 2 * i + 1)
                dve.scalar_tensor_tensor(out=xt[i % 2][:], in0=xt[i % 2][:], scalar=x_std[:, i:i + 1],
                                         in1=gain[:], op0=ALU.mult, op1=ALU.mult).then_inc(d_x, 1)

            def hT_lo(i):
                for half in range(2):
                    m = 2 * i + half
                    hi = hT[:, 0, 4 * half:4 * half + 4, tk(i)]
                    dve.wait_ge(t_hi, m + 1)
                    dve.tensor_tensor(hT[:, 1, 4 * half:4 * half + 4, tk(i)],
                                      bank[3 + m % 4][:].rearrange("p (k t) -> p k t", k=4), f(hi),
                                      ALU.subtract).then_inc(t_free[m % 4], 1)

            x_norm(0)
            x_norm(1)
            hT_lo(0)
            split_lo(0)
            split_lo(1)
            x_norm(2)
            hT_lo(1)
            split_lo(2)
            split_lo(3)

            def tbank(m):
                return bank[3 + m % 4][:].rearrange("p (k t) -> p k t", k=4)

            def gate_mul(i):
                m = TJ[GATE_B] + i
                dve.wait_ge(pe_t, m + 1)
                dve.tensor_tensor(convT[:, :, tk(i)], tbank(m), convT[:, :, tk(i)],
                                  ALU.mult).then_inc(t_free[m % 4], 1)

            def qk_out(b, i):
                m = TJ[b] + i
                dve.wait_ge(pe_t, m + 1)
                if b == Q_B:
                    if i == 0:
                        dve.wait_ge(b_st, 16)
                    ins = dve.tensor_scalar(qT[:, :, tk(i)], tbank(m), colv[:, 0:1], HD ** -0.5,
                                            ALU.mult, ALU.mult)
                else:
                    ins = dve.tensor_scalar(kT[:, :, tk(i)], tbank(m), colv[:, 1:2], None, ALU.mult)
                ins.then_inc(t_free[m % 4], 1)

            for b in range(6):
                for i in range(TILES):
                    n = TILES * b + i
                    if b == CONV_B:
                        if i + 3 < TILES:
                            x_norm(i + 3)
                        if i + 2 < TILES:
                            hT_lo(i + 2)
                    elif b == X_B:
                        dve.wait_ge(pe_acc, n + 1)
                        dve.tensor_tensor(u_tok[:, i], bank[n % 3][:], u_tok[:, i],
                                          ALU.mult).then_inc(acc_free[n % 3], 1)
                    elif b in (Q_B, K_B):
                        r = n - TILES * Q_B
                        ss = qk_ss[:, 8 * r:8 * r + 8]
                        if r == 0:
                            gate_mul(TILES - 1)
                        elif i == 0:
                            qk_out(Q_B, TILES - 1)
                        dve.wait_ge(a_sq, r + 1)
                        dve.reduce_sum(ss, sq_tmp[:].rearrange("p (m d) -> p m d", m=MAPS),
                                       AX_X).then_inc(d_ss, 1)
                        if i >= 1:
                            qk_out(b, i - 1)
                        dve.wait_ge(a_sd, r + 1)
                        link(dve.reciprocal(ss, ss))
                        if r >= 2:
                            dve.wait_ge(pe_t, TJ[Q_B] + r - 1)
                        else:
                            dve.wait_ge(pe_t, TJ[GATE_B] + 5 + r)
                        dve.tensor_tensor(tok_tmp[i % 2][:].rearrange("p (m d) -> p m d", m=MAPS),
                                          bank[n % 3][:].rearrange("p (m d) -> p m d", m=MAPS),
                                          ss.unsqueeze(2).broadcast_to([P, MAPS, HD]),
                                          ALU.mult).then_inc(acc_free[n % 3], 1)
                    elif b == GATE_B and i >= 1:
                        gate_mul(i - 1)
                    elif b == V_B and i == 0:
                        qk_out(K_B, TILES - 1)
                    if i < 4:
                        split_lo(4 * (b + 1) + i)
                if b == X_B:
                    for m in range(TJ[X_B] + 2, TJ[X_B] + 6):
                        t_ready(dve, m)
                    for c in range(4):
                        link(dve.tensor_scalar(convT[:, c], uT[:, c], colv[:, 3 + 4 + c:4 + 4 + c],
                                               None, ALU.mult))
                        s0 = 0
                        for s in SEQS:
                            e0 = s0 + s
                            for tap, dst, src in ((0, (s0 + 1, e0), (s0, e0 - 1)),
                                                  (2, (s0, e0 - 1), (s0 + 1, e0))):
                                link(dve.scalar_tensor_tensor(
                                    out=convT[:, c, dst[0]:dst[1]], in0=uT[:, c, src[0]:src[1]],
                                    scalar=colv[:, 3 + 4 * tap + c:4 + 4 * tap + c],
                                    in1=convT[:, c, dst[0]:dst[1]], op0=ALU.mult, op1=ALU.add))
                            s0 = e0
                if b == CONV_B:
                    dve.wait_ge(a_lam, 1)
                    link(dve.tensor_tensor(lam[:, 2:3], lam[:, 1:2], lam[:, 0:1], ALU.subtract))
                    link(dve.tensor_scalar(lam[:, 2:3], lam[:, 2:3], LAMBDA_INIT, None, ALU.subtract))

            def scores(w):
                h, i = ITEMS[w]
                nk = keys(i)[1]
                qt = i if i < PROMPT_TILES else i - PROMPT_TILES
                c0 = 384 - P * qt
                if i == 0:
                    dve.wait_ge(toep_ld[h % 2], 16 * (h // 2 + 1))
                if w >= 2:
                    dve.wait_ge(pe_at, w - 1)
                for m in range(2):
                    dve.wait_ge(pe_s, 2 * w + m + 1)
                    dve.tensor_tensor_reduce(s_sb[w % 2][m][:, 0:nk],
                                             bank[2 * (w % 2) + m][:, 0:nk],
                                             toep[h % 2][:, m, c0:c0 + nk], 1.0, -3.0e38, ALU.add,
                                             ALU.max, mx[:, 2 * w + m:2 * w + m + 1]).then_inc(d_s, 1)
                dve.wait_ge(d_s, 2 * w + 2)
                dve.tensor_scalar(nmx[:, 2 * w:2 * w + 2], mx[:, 2 * w:2 * w + 2], -1.0, None,
                                  ALU.mult).then_inc(d_nm, 1)

            def combine(w):
                nk = keys(ITEMS[w][1])[1]
                dve.wait_ge(a_e, 2 * w + 2)
                link(dve.reciprocal(rz[:, 2 * w:2 * w + 2], Z[:, 2 * w:2 * w + 2]))
                link(dve.scalar_tensor_tensor(out=ratio[:, w:w + 1], in0=Z[:, 2 * w:2 * w + 1],
                                              scalar=lam[:, 2:3], in1=rz[:, 2 * w + 1:2 * w + 2],
                                              op0=ALU.mult, op1=ALU.mult))
                s0, s1 = (s_sb[w % 2][m][:, 0:nk] for m in range(2))
                dve.scalar_tensor_tensor(out=s0, in0=s1, scalar=ratio[:, w:w + 1], in1=s0,
                                         op0=ALU.mult, op1=ALU.add).then_inc(d_a, 1)

            def o_out(w):
                h, i = ITEMS[w]
                o_ = o_tok[:, i, h * VD:(h + 1) * VD]
                dve.wait_ge(pe_o, w + 1)
                dve.tensor_scalar(o_, bank[6 + w % 2][:, 0:VD], rz[:, 2 * w:2 * w + 1], None,
                                  ALU.mult).then_inc(d_o, 1)
                dve.wait_ge(d_o, w + 1)
                if w >= 1:
                    dve.wait_ge(d_oss, w)
                dve.tensor_tensor_reduce(ojunk[:], o_, o_, 1.0, 0.0, ALU.mult, ALU.add,
                                         o_ssq[:, w:w + 1]).then_inc(d_oss, 1)

            for w in range(NI + 3):
                if w < NI:
                    scores(w)
                if 1 <= w <= NI:
                    combine(w - 1)
                if w >= 3:
                    o_out(w - 3)
                if w < 4:
                    split_lo(OUT0 + 4 + w)

            dve.wait_ge(a_os, 1)
            link(dve.reciprocal(o_ssq[:], o_ssq[:]))
            ors = o_ssq[:].rearrange("p (h i) -> p i h", h=HEADS)

            def o_norm(i):
                ot = o_tok[:, i].rearrange("p (h d) -> p h d", h=HEADS)
                dve.tensor_tensor(ot, ot, ors[:, i].unsqueeze(2).broadcast_to([P, HEADS, VD]),
                                  ALU.mult).then_inc(d_on, 1)

            def mix_lo(i):
                dve.wait_ge(a_mix, i + 1)
                for_lo = mixA[1][:, :, tk(i)]
                b4 = bank[4 + i % 2]
                dve.scalar_tensor_tensor(out=for_lo, in0=b4[:].rearrange("p (k t) -> p k t", k=4),
                                         scalar=gs[:], in1=f(mixA[0][:, :, tk(i)]),
                                         op0=ALU.mult, op1=ALU.subtract).then_inc(d_mix, 1)
                dve.wait_ge(a_mixc, i + 1)
                dve.tensor_tensor(mixC[1][:, :, tk(i)], convT[:, :, tk(i)], f(mixC[0][:, :, tk(i)]),
                                  ALU.subtract).then_inc(d_mixc, 1)

            o_norm(0)
            for i in range(TILES):
                if i + 1 < TILES:
                    o_norm(i + 1)
                mix_lo(i)

            for i in range(TILES):
                if i == 0:
                    dve.wait_ge(gain_ld, 32)
                    dve.wait_ge(d_mixc, TILES)
                dve.wait_ge(xr_ld[i % 2], 16 * (i // 2 + 1))
                for half in range(2):
                    c = slice(half * N, (half + 1) * N)
                    dve.wait_ge(pe_wo, 2 * i + half + 1)
                    dve.tensor_tensor(x2[i][:, c], bank[2 * (i % 2) + half][:], xr[i % 2][:, c],
                                      ALU.add).then_inc(d_x2, 1)
                dve.wait_ge(a_x2, 2 * i + 2)
                link(dve.reciprocal(x2_ssq[:, i:i + 1], x2_ssq[:, i:i + 1]))
                dve.scalar_tensor_tensor(out=h2[i][:], in0=x2[i][:], scalar=x2_ssq[:, i:i + 1],
                                         in1=gain[:], op0=ALU.mult, op1=ALU.mult).then_inc(d_h2, 1)
            for u in range(PLE0, MOE0):
                split_lo(u)
            dve.wait_ge(a_p, 1)
            dve.tensor_tensor(pTs[1][:], p_raw[:], f(pTs[0][:]), ALU.subtract).then_inc(d_p, 1)

            def bc(ap, shape):
                return ap.broadcast_to([P, *shape])

            def first_max(out, score, vals, top):
                n4 = [TILES, 4]
                link(dve.tensor_tensor(score[:], vals, bc(top[:].unsqueeze(2), n4), ALU.is_equal))
                link(dve.tensor_tensor(score[:], score[:], bc(cst[:, C_DESC:C_DESC + 4].unsqueeze(1), n4),
                                       ALU.mult))
                link(dve.reduce_max(r_gs[:], score[:], AX_X))
                link(dve.tensor_tensor(out[:], score[:], bc(r_gs[:].unsqueeze(2), n4), ALU.is_equal))

            dve.wait_ge(pe_r, TILES)
            link(dve.tensor_tensor(r_lg[:], bank[4][:, 0:TILES * ROUTES].rearrange(
                "p (i r) -> p i r", i=TILES), bc(bias_row[:].unsqueeze(1), [TILES, ROUTES]), ALU.add))
            lg, le = r_lg[:, :, 0:G], r_lg[:, :, G:ROUTES]
            link(dve.reduce_max(r_gm[:], lg, AX_X))
            dve.tensor_tensor(r_ge[:], lg, bc(r_gm[:].unsqueeze(2), [TILES, G]),
                              ALU.subtract).then_inc(d_lg, 1)
            first_max(r_oh, r_sc, lg, r_gm)
            link(dve.tensor_tensor(
                r_O[0][:], le.rearrange("p i (g e) -> p i g e", g=G),
                bc(r_oh[:].unsqueeze(3), [TILES, G, EPG]), ALU.mult))
            link(dve.reduce_sum(r_sel[:], r_O[0][:].rearrange("p i g e -> p i e g"), AX_X))
            link(dve.reduce_max(r_m1[:], r_sel[:], AX_X))
            first_max(r_o1, r_sc, r_sel[:], r_m1)
            link(dve.scalar_tensor_tensor(out=r_sel[:], in0=r_o1[:], scalar=-1.0e30, in1=r_sel[:],
                                          op0=ALU.mult, op1=ALU.add))
            link(dve.reduce_max(r_m2[:], r_sel[:], AX_X))
            dve.tensor_tensor(r_e2[:], r_m2[:], r_m1[:], ALU.subtract).then_inc(d_lg, 1)
            first_max(r_o2, r_sc, r_sel[:], r_m2)
            for O, pick in zip(r_O, (r_o1, r_o2)):
                link(dve.tensor_tensor(O[:], bc(r_oh[:].unsqueeze(3), [TILES, G, EPG]),
                                       bc(pick[:].unsqueeze(2), [TILES, G, EPG]), ALU.mult))
            flat = [O[:].rearrange("p i g e -> p i (g e)") for O in r_O]
            link(dve.tensor_tensor(r_M[:, 0:TILES], flat[0], flat[1], ALU.add))
            link(dve.memset(r_C[:, 0], 0.0))
            for i in range(1, TILES):
                link(dve.tensor_tensor(r_C[:, i], r_C[:, i - 1], r_M[:, i - 1], ALU.add))
            dve.tensor_tensor(r_M[:, TILES], r_C[:, TILES - 1], r_M[:, TILES - 1],
                              ALU.add).then_inc(d_m, 1)
            dve.wait_ge(a_g, 1)
            link(dve.reduce_sum(r_gs[:], r_ge[:], AX_X))
            dve.wait_ge(a_e2, 1)
            link(dve.scalar_tensor_tensor(out=wgt[:, 0:TILES], in0=r_e2[:], scalar=1.0, in1=r_gs[:],
                                          op0=ALU.add, op1=ALU.mult))
            link(dve.reciprocal(wgt[:, 0:TILES], wgt[:, 0:TILES]))
            link(dve.tensor_tensor(wgt[:, TILES:2 * TILES], wgt[:, 0:TILES], r_e2[:], ALU.mult))
            dve.wait_ge(pe_rk, 1)
            link(dve.tensor_copy(r_cnt[:], bank[5][:, TILES * E:(TILES + 1) * E]))
            link(dve.tensor_tensor(r_ov[:], bc(r_cnt[:].unsqueeze(2), [E, 6]),
                                   bc(cst[:, C_THR:C_THR + 6].unsqueeze(1), [E, 6]), ALU.is_gt))
            link(dve.reduce_sum(r_b[:], r_ov[:], AX_X))
            link(dve.tensor_tensor_scan(r_inc[:], cst[:, C_ONE:C_ONE + E], r_b[:], 0.0, ALU.mult, ALU.add))
            link(dve.tensor_tensor(r_base[:], r_inc[:], r_b[:], ALU.subtract))
            link(dve.scalar_tensor_tensor(out=r_base[:], in0=r_base[:], scalar=float(P),
                                          in1=cst[:, C_K15:C_K15 + E], op0=ALU.mult, op1=ALU.add))
            te = [TILES, E]
            rank = bank[5][:, 0:TILES * E].rearrange("p (i e) -> p i e", i=TILES)
            link(dve.tensor_scalar(r_big[:], rank, float(P), None, ALU.is_ge))
            link(dve.tensor_tensor(r_big[:], r_big[:], bc(r_base[:].unsqueeze(1), te), ALU.mult))
            link(dve.tensor_tensor(r_slot[:], rank, r_big[:], ALU.add))
            link(dve.tensor_tensor(r_slot[:], r_slot[:], bc(cst[:, C_E128:C_E128 + E].unsqueeze(1), te),
                                   ALU.add))
            for j in range(2):
                link(dve.tensor_tensor(r_t[:], r_slot[:], flat[j], ALU.mult))
                link(dve.reduce_sum(r_gm[:], r_t[:], AX_X))
                link(dve.tensor_copy(slot_u[:, j * TILES:(j + 1) * TILES], r_gm[:]))
            link(dve.tensor_tensor(r_et[:], bc(r_inc[:].unsqueeze(1), [OVER_TILES, E]),
                                   bc(cst[:, C_T:C_T + OVER_TILES].unsqueeze(2), [OVER_TILES, E]),
                                   ALU.is_le))
            link(dve.reduce_sum(r_ef[:, 0:OVER_TILES], r_et[:], AX_X))
            link(dve.tensor_scalar(r_ef[:, 0:OVER_TILES], r_ef[:, 0:OVER_TILES], float(E - 1), None,
                                   ALU.min))
            link(dve.tensor_scalar(r_ef[:, OVER_TILES:OVER_TILES + 1], r_inc[:, E - 1:E], float(E - 1),
                                   None, ALU.add))
            link(dve.tensor_copy(etab[:, 0:E], cst[:, C_T:C_T + E]))
            link(dve.tensor_copy(etab[:, E:MOE_TILES], r_ef[:, 0:OVER_TILES]))
            dve.tensor_copy(last_tile[:], r_ef[:, OVER_TILES:OVER_TILES + 1]).then_inc(d_route, 1)

            for i in range(TILES):
                dve.wait_ge(ach, TILES + i + 1)
                dve.reciprocal(e_ssq[:, i:i + 1], e_ssq[:, i:i + 1]).then_inc(d_ple, 1)
                split_lo(MOE0 + i)

            dve.wait_ge(d_route, 1)
            last = dve.value_load(last_tile[0:1, 0:1], min_val=E - 1, max_val=MOE_TILES - 1)

            def xT_lo(half, t=None):
                c = half + 1 if t is None else t * 2 + (3 + half)
                dve.wait_ge(a_xt, c)
                dve.tensor_tensor(xgT[1][:, 4 * half:4 * half + 4],
                                  bank[1 + half][:].rearrange("p (k t) -> p k t", k=4),
                                  f(xgT[0][:, 4 * half:4 * half + 4]), ALU.subtract).then_inc(d_xt, 1)

            def act_mul(t):
                dve.wait_ge(a_si, t + 1)
                dve.tensor_tensor(act_t[:], bank[0][:, DE:2 * DE], sg[:], ALU.mult).then_inc(d_act, 1)

            def actT_lo(t):
                dve.wait_ge(a_aT2, t + 1)
                dve.tensor_tensor(actT[1][:], bank[3][:, 0:DE].rearrange("p (k t) -> p k t", k=2),
                                  f(actT[0][:]), ALU.subtract).then_inc(d_aT2, 1)

            def y_right(t):
                dve.wait_ge(pe_y, t * 2 + 2)
                dve.wait_ge(y_free[1], t + 1)
                dve.tensor_copy(yb[:, 1], bank[5][:]).then_inc(d_y, 1)

            def moe_lo(j, t):
                s, w = (MOE0 + j) % RS, (MOE0 + j) % WS
                dve.wait_ge(hi_done, t * 6 + (MOE0 + 6 + j + 1))
                dve.tensor_tensor(W[:, w, 1], RAW[:, s], f(W[:, w, 0]), ALU.subtract).then_inc(lo_done, 1)

            xT_lo(0)
            xT_lo(1)
            dve.sem_inc(d_act, 1)
            dve.sem_inc(d_aT2, 1)
            dve.sem_inc(d_y, 1)
            with dve.Fori(0, last) as t:
                for j in range(3):
                    moe_lo(j, t)
                act_mul(t)
                xT_lo(0, t)
                actT_lo(t)
                xT_lo(1, t)
                for j in range(3, 5):
                    moe_lo(j, t)
                y_right(t)
                moe_lo(5, t)
            act_mul(last)
            actT_lo(last)
            y_right(last)
            for g in range(FIN_UNITS):
                split = MOE0 + g
                dve.wait_ge(hi_done, last * 6 + (split + 7))
                dve.tensor_tensor(W[:, g % WS, 1], RAW[:, split % RS], f(W[:, g % WS, 0]),
                                  ALU.subtract).then_inc(lo_done, 1)

            def x3(i):
                dve.wait_ge(pk_ld[i % 2], 32 * (i // 2 + 1))
                for j, buf in ((0, ga), (1, gb)):
                    c = j * TILES + i
                    ins = dve.scalar_tensor_tensor(out=x2[i][:], in0=buf[i % 2][:],
                                                   scalar=wgt[:, c:c + 1], in1=x2[i][:],
                                                   op0=ALU.mult, op1=ALU.add)
                    if j == 0:
                        link(ins)
                    else:
                        ins.then_inc(d_x3, 1)

            def x3T_lo(i):
                for half in range(2):
                    dve.wait_ge(a_x3, 2 * i + half + 1)
                    dve.tensor_tensor(x3T[i % 2][1][:, 4 * half:4 * half + 4],
                                      bank[6 + half][:].rearrange("p (k t) -> p k t", k=4),
                                      f(x3T[i % 2][0][:, 4 * half:4 * half + 4]),
                                      ALU.subtract).then_inc(d_x3t, 1)

            dve.wait_ge(g_ple, 2 * TILES)
            x3(0)
            x3T_lo(0)
            for i in range(TILES):
                if i + 1 < TILES:
                    x3(i + 1)
                    x3T_lo(i + 1)
                dve.wait_ge(a_g2, 2 * i + 2)
                if i >= 1:
                    dve.wait_ge(o_st, 16 * i)
                link(dve.tensor_tensor(outb[:], sig[:], ple[i][:], ALU.mult))
                dve.tensor_tensor(outb[:], outb[:], x2[i][:], ALU.add).then_inc(d_out, 1)

        @block.tensor
        def _(pe):
            def turn(out, src, k, inc, first=0):
                for q in range(k):
                    ins = pe.transpose(out[:, q * P:(q + 1) * P], src[:, (first + q) * P:(first + q + 1) * P],
                                       ident)
                ins.then_inc(inc, 1)

            def turn_back(out, src, inc):
                for q in range(4):
                    ins = pe.matmul(out[:, q * P:(q + 1) * P], src[:, q * P:(q + 1) * P],
                                    cst[:, C_J:C_J + P], start=True, stop=True)
                ins.then_inc(inc, 1)

            def t_bank(m):
                if m >= 4:
                    pe.wait_ge(t_free[m % 4], m // 4)
                return bank[3 + m % 4]

            def turn_h(i):
                pe.wait_ge(d_x, 2 * i + 2)
                for half in range(2):
                    turn(t_bank(2 * i + half), xt[i % 2], 4, pe_t, 4 * half)

            pe.wait_ge(c_ld, 16 * 7)
            turn_h(0)
            turn_h(1)
            for b in range(6):
                for i in range(TILES):
                    n = TILES * b + i
                    if b == 0:
                        t_ready(pe, 2 * i)
                        t_ready(pe, 2 * i + 1)
                    if n >= 3:
                        pe.wait_ge(acc_free[n % 3], n // 3)
                    for k in range(KD):
                        u = 4 * b + k // 2
                        if i == 0 and k % 2 == 0:
                            pe.wait_ge(lo_done, u + 1)
                        w = W[:, u % WS]
                        ins = three(bank[n % 3][:], hT[:, 0, k, tk(i)], hT[:, 1, k, tk(i)],
                                    w[:, 0, k % 2], w[:, 1, k % 2], k == 0, k == KD - 1)
                        if k == KD - 1:
                            ins.then_inc(pe_acc, 1)
                        elif i == TILES - 1 and k % 2:
                            ins.then_inc(w_used, 1)
                    if b == 0 and i + 2 < TILES:
                        turn_h(i + 2)
                    pb, pi = divmod(n - 1, TILES)
                    if n >= 1 and pb in TJ:
                        m = TJ[pb] + pi
                        src = u_tok[:, pi] if pb == X_B else tok_tmp[pi % 2]
                        out = t_bank(m)
                        pe.wait_ge(acc_free[(n - 1) % 3], (n - 1) // 3 + 1)
                        if pb == Q_B:
                            turn_back(out, src, pe_t)
                        else:
                            turn(out, src, 4, pe_t)
                if b == CONV_B:
                    for half in range(2):
                        if half:
                            pe.wait_ge(a_b, half)
                        pe.matmul(bank[7][0:MAPS], relb[0:BUCKETS, :], hot_sb[:, half * N:(half + 1) * N],
                                  start=True, stop=True).then_inc(pe_b, 1)

            for n in range(33, 36):
                pe.wait_ge(acc_free[n % 3], n // 3 + 1)
            for m in range(32, 36):
                t_ready(pe, m)

            def scores(w):
                h, i = ITEMS[w]
                k0, nk = keys(i)
                pe.wait_ge(p_pad, 2 * w + 2)
                if w >= 2:
                    pe.wait_ge(d_s, 2 * (w - 1))
                for m in range(2):
                    pe.matmul(bank[2 * (w % 2) + m][:, 0:nk], pad[w % 2][:, m], kT[:, h, k0:k0 + nk],
                              start=True, stop=True).then_inc(pe_s, 1)

            def turn_a(w):
                nk = keys(ITEMS[w][1])[1]
                pe.wait_ge(d_a, w + 1)
                if w >= 2:
                    pe.wait_ge(a_at, w - 1)
                turn(bank[4 + w % 2], s_sb[w % 2][0], nk // P, pe_at)

            def pv(w):
                h, i = ITEMS[w]
                k0, nk = keys(i)
                pe.wait_ge(a_at, w + 1)
                if w >= 2:
                    pe.wait_ge(d_o, w - 1)
                for q in range(nk // P):
                    ins = pe.matmul(bank[6 + w % 2][:, 0:VD], aT[w % 2][:, q * P:(q + 1) * P],
                                    v[:, k0 // P + q, h * VD:(h + 1) * VD],
                                    start=(q == 0), stop=(q == nk // P - 1))
                ins.then_inc(pe_o, 1)

            for w in range(NI + 3):
                if w < NI:
                    scores(w)
                if 2 <= w < NI + 2:
                    turn_a(w - 2)
                if w >= 3:
                    pv(w - 3)

            def turn_o(i):
                pe.wait_ge(d_on, i + 1)
                if i >= 2:
                    pe.wait_ge(d_mix, i - 1)
                turn_back(bank[4 + i % 2], o_tok[:, i], pe_ot)

            def out_proj(i, half):
                if half == 0:
                    pe.wait_ge(d_mixc, i + 1)
                if i >= 2:
                    pe.wait_ge(d_x2, 2 * (i - 2) + half + 1)
                for k in range(KD):
                    u = OUT0 + 4 * half + k // 2
                    if i == 0 and k % 2 == 0:
                        pe.wait_ge(lo_done, u + 1)
                    src = mixA if k < 4 else mixC
                    w = W[:, u % WS]
                    ins = three(bank[2 * (i % 2) + half][:], src[0][:, k % 4, tk(i)],
                                src[1][:, k % 4, tk(i)], w[:, 0, k % 2], w[:, 1, k % 2],
                                k == 0, k == KD - 1)
                    if k == KD - 1:
                        ins.then_inc(pe_wo, 1)
                    elif i == TILES - 1 and k % 2:
                        ins.then_inc(w_used, 1)

            def turn_h2(i):
                pe.wait_ge(d_h2, i + 1)
                for half in range(2):
                    if i >= 1:
                        pe.wait_ge(a_h2, 2 * (i - 1) + half + 1)
                    turn(bank[6 + half], h2[i], 4, pe_h2, 4 * half)

            def router(i):
                pe.wait_ge(a_h2, 2 * i + 2)
                for k in range(KD):
                    ins = pe.matmul(bank[4][:, i * ROUTES:(i + 1) * ROUTES], h2T[:, k], wr[:, k],
                                    start=(k == 0), stop=(k == KD - 1))
                ins.then_inc(pe_r, 1)

            for i in range(3):
                turn_o(i)
            for i in range(TILES):
                out_proj(i, 0)
                if i == 0:
                    for j in range(3, TILES):
                        turn_o(j)
                    pe.wait_ge(d_mix, TILES)
                if i >= 1:
                    turn_h2(i - 1)
                out_proj(i, 1)
                if i >= 1:
                    router(i - 1)
            turn_h2(TILES - 1)

            def ple_proj(i):
                for half in range(2):
                    u = PLE0 + half
                    if i == 0:
                        pe.wait_ge(lo_done, u + 1)
                    if i < 2:
                        pe.wait_ge(d_x2, 2 * (TILES - 2 + i) + half + 1)
                    else:
                        pe.wait_ge(a_ple, 3 * (i - 2) + half + 1)
                    w = W[:, u % WS]
                    for k in range(2):
                        ins = three(bank[2 * (i % 2) + half][:], pTs[0][:, k, tk(i)],
                                    pTs[1][:, k, tk(i)], w[:, 0, k], w[:, 1, k], k == 0, k == 1)
                    ins.then_inc(pe_ple, 1)

            router(TILES - 1)
            pe.wait_ge(d_p, 1)
            ple_proj(0)
            ple_proj(1)
            pe.wait_ge(d_m, 1)
            rk = bank[5]
            pe.matmul(rk[:, 0:TILES * E], cst[:, C_U:C_U + P], r_M[:, 0:TILES].rearrange("p i e -> p (i e)"),
                      start=True, stop=False)
            pe.matmul(rk[:, 0:TILES * E], cst[:, C_ONE:C_ONE + P], r_C[:].rearrange("p i e -> p (i e)"),
                      start=False, stop=True)
            pe.matmul(rk[:, TILES * E:(TILES + 1) * E], cst[:, C_ONE:C_ONE + P], r_M[:, TILES],
                      start=True, stop=True).then_inc(pe_rk, 1)
            for i in range(2, TILES):
                ple_proj(i)

            pe.wait_ge(d_route, 1)
            last = pe.value_load(last_tile[0:1, 0:1], min_val=E - 1, max_val=MOE_TILES - 1)

            def turn_x(half, t=None):
                if t is None:
                    pe.wait_ge(xg_ld, 16)
                else:
                    pe.wait_ge(xg_ld, t * 16 + 32)
                    pe.wait_ge(d_xt, t * 2 + (half + 1))
                turn(bank[1 + half], xg, 4, pe_xt, 4 * half)

            def gate_up(t):
                pe.wait_ge(d_xt, t * 2 + 2)
                pe.wait_ge(d_act, t + 1)
                for k in range(KD):
                    u = MOE0 + k // 2
                    if k % 2 == 0:
                        pe.wait_ge(lo_done, t * 6 + (u + 1))
                    w = W[:, u % WS]
                    ins = three(bank[0][:], xgT[0][:, k], xgT[1][:, k], w[:, 0, k % 2], w[:, 1, k % 2],
                                k == 0, k == KD - 1)
                    if k == KD - 1:
                        ins.then_inc(pe_gu, 1)
                    elif k % 2:
                        ins.then_inc(w_used, 1)

            def turn_act(t):
                pe.wait_ge(d_act, t + 2)
                pe.wait_ge(d_aT2, t + 1)
                turn(bank[3], act_t, 2, pe_aT2)

            def down(t):
                pe.wait_ge(d_aT2, t + 2)
                for half, free in ((0, a_y), (1, d_y)):
                    u = MOE0 + 4 + half
                    pe.wait_ge(free, t + 1)
                    pe.wait_ge(lo_done, t * 6 + (u + 1))
                    w = W[:, u % WS]
                    for k in range(2):
                        ins = three(bank[4 + half][:], actT[0][:, k], actT[1][:, k], w[:, 0, k],
                                    w[:, 1, k], k == 0, k == 1)
                    ins.then_inc(pe_y, 1)

            pe.wait_ge(a_ple, 3 * TILES)
            turn_x(0)
            turn_x(1)
            with pe.Fori(0, last) as t:
                gate_up(t)
                turn_x(0, t)
                turn_act(t)
                turn_x(1, t)
                down(t)
            gate_up(last)
            turn_act(last)
            down(last)

            def turn_x3(i):
                pe.wait_ge(d_x3, i + 1)
                for half in range(2):
                    if i >= 1:
                        pe.wait_ge(d_x3t, 2 * (i - 1) + half + 1)
                    turn(bank[6 + half], x2[i], 4, pe_x3, 4 * half)

            def gate(i, half):
                if half == 0:
                    pe.wait_ge(d_x3t, 2 * i + 2)
                if i >= 2:
                    pe.wait_ge(a_g2, 2 * (i - 2) + half + 1)
                for k in range(KD):
                    g = 4 * half + k // 2
                    if i == 0 and k % 2 == 0:
                        pe.wait_ge(lo_done, last * 6 + (MOE0 + g + 7))
                    w = W[:, g % WS]
                    ins = three(bank[2 * (i % 2) + half][:], x3T[i % 2][0][:, k], x3T[i % 2][1][:, k],
                                w[:, 0, k % 2], w[:, 1, k % 2], k == 0, k == KD - 1)
                ins.then_inc(pe_g, 1)

            turn_x3(0)
            for i in range(TILES):
                gate(i, 0)
                if i + 1 < TILES:
                    turn_x3(i + 1)
                gate(i, 1)


def units(w):
    k, n = w.shape
    return np.ascontiguousarray(
        w.reshape(k // 256, 2, P, n // N, N).transpose(3, 0, 2, 1, 4).reshape(-1, P, 2, N))


def kernel(**inputs):
    import concourse.bacc as _bacc
    from concourse.bass_utils import run_bass_kernel_spmd as _run

    a = {k: np.asarray(v) for k, v in inputs.items()}
    x = np.concatenate([a["x_prompt"][0], a["x_sample"][0]])
    p = np.concatenate([a["p_prompt"][0, 0], a["p_sample"][0, 0]])
    w_in = a["w_in"][0]
    order = [4, 5, 3, 0, 1, 2]
    w_in = np.concatenate([w_in[:, N * b:N * (b + 1)] for b in order], axis=1)
    gu = a["w_gate_up"][0].reshape(E, 4, 2, P, N).transpose(0, 1, 3, 2, 4)
    dn = a["w_down"][0].reshape(E, 2, P, 2, N).transpose(0, 3, 2, 1, 4)
    conv = a["conv_w"][0].reshape(3, 4, P).transpose(2, 0, 1).reshape(P, 12)
    cst, hot = constants()
    data = {
        "x": x,
        "pT": p.T.reshape(2, P, TOK).transpose(1, 0, 2),
        "w_in": units(w_in),
        "w_out": units(a["w_out"][0]),
        "w_ple": units(a["w_ple_proj"][0]),
        "w_moe": np.concatenate([gu, dn], axis=1),
        "w_gate": units(a["w_ple_gate"][0]),
        "w_route": np.concatenate([a["w_group"][0], a["w_erouter"][0]], axis=1).reshape(
            KD, P, ROUTES).transpose(1, 0, 2),
        "gains": np.stack([np.broadcast_to(a[k][0], (P, D)) for k in ("norm_mix", "norm_ffn", "ple_norm")]),
        "cols": np.concatenate([np.concatenate([a["q_norm"][0]] * 2)[:, None],
                                np.concatenate([a["k_norm"][0]] * 2)[:, None],
                                a["attn_sub_norm"][0][:, None], conv], axis=1),
        "rows": np.broadcast_to(np.concatenate([
            a["lambda_q1"][0], a["lambda_k1"][0], a["lambda_q2"][0], a["lambda_k2"][0],
            a["b_group"][0], a["b_erouter"][0]]), (P, 4 * HD + ROUTES)),
        "rel_bias": a["rel_bias"],
        "consts": cst,
        "hot": hot,
    }
    nc = _bacc.Bacc("TRN2", target_bir_lowering=False, num_devices=1)
    arrays, args = {}, {}
    for name, arr in data.items():
        arr = np.ascontiguousarray(arr)
        arrays[f"in_{name}"] = arr
        args[name] = nc.dram_tensor(f"in_{name}", arr.shape, mybir.dt.from_np(arr.dtype),
                                    kind="ExternalInput").ap()
    for name, s in (("y_prompt", SEQS[0]), ("y_sample", SEQS[1])):
        args[name] = nc.dram_tensor(f"out_{name}", (s, D), F32, kind="ExternalOutput").ap()
    build(nc, **args)
    r = _run(nc, [arrays], core_ids=[0])
    return tuple(np.asarray(r.results[0][f"out_{n}"]).reshape(1, s, D)
                 for n, s in (("y_prompt", SEQS[0]), ("y_sample", SEQS[1])))
```

```python
from contextlib import ExitStack

import numpy as np

import concourse.bass as bass
from concourse import mybir

F32 = mybir.dt.float32
F32R = mybir.dt.float32r
I32 = mybir.dt.int32
U32 = mybir.dt.uint32
ALU = mybir.AluOpType
ACT = mybir.ActivationFunctionType
AX_X = mybir.AxisListType.X

P = 128
D = 1024
KD = D // P
SEQS = (512, 256)
TOK = sum(SEQS)
TILES = TOK // P
PROMPT_TILES = SEQS[0] // P
D_ATT = 512
HEADS = 4
MAPS = 2 * HEADS
HD = 64
VD = 128
BUCKETS = 32
MAX_DISTANCE = 128
G = 4
EPG = 4
E = G * EPG
DE = 256
PLE = 256
EPS = 1e-6
LAMBDA_INIT = 0.2
N = 512
ROUTES = G + E

PAIRS = 2 * TOK
OVER_TILES = PAIRS // (P + 1)
MOE_TILES = E + OVER_TILES

CONV_B, X_B, GATE_B, Q_B, K_B, V_B = range(6)
IN_UNITS, OUT_UNITS, PLE_UNITS, MOE_UNITS, FIN_UNITS = 24, 8, 2, 6, 8
OUT0 = IN_UNITS
PLE0 = OUT0 + OUT_UNITS
MOE0 = PLE0 + PLE_UNITS
WS = 8
RS = 6

GW = 896
REL = 1024

C_ID, C_U, C_ONE, C_J, C_DESC, C_E128, C_K15, C_THR, C_T = 0, 128, 256, 384, 512, 516, 532, 548, 554
L_IOTA, L_SLOT, L_TOK = 0, P, P + MOE_TILES + 1
L_N = L_TOK + 2 * TILES
C_N = C_T + E


def constants():
    late = np.zeros((P, L_N), np.float32)
    late[:, L_IOTA:L_IOTA + P] = np.arange(P)
    late[:, L_SLOT:L_TOK] = P * np.arange(MOE_TILES + 1)
    late[:, L_TOK:] = np.arange(P)[:, None] + P * np.tile(np.arange(TILES), 2)
    c = np.zeros((P, C_N), np.float32)
    c[:, C_ID:C_ID + P] = np.eye(P)
    c[:, C_U:C_U + P] = np.triu(np.ones((P, P)), 1)
    c[:, C_ONE:C_ONE + P] = 1
    c[:, C_J:C_J + P] = np.eye(P)[::-1]
    c[:, C_DESC:C_DESC + 4] = [4, 3, 2, 1]
    c[:, C_E128:C_E128 + E] = P * np.arange(E)
    c[:, C_K15:C_K15 + E] = P * (E - 1 - np.arange(E))
    c[:, C_THR:C_THR + 6] = P * np.arange(1, 7)
    c[:, C_T:C_T + E] = np.arange(E)
    rel = np.arange(REL) - REL // 2
    n = np.abs(rel)
    starts = [1, 2, 3, 4, 5, 6, 7, 8, 12, 16, 23, 32, 46, 64, 91]
    bucket = sum((n >= s).astype(int) for s in starts) + np.where(rel > 0, BUCKETS // 2, 0)
    hot = (np.arange(BUCKETS)[:, None] == bucket[None, :]).astype(np.float32)
    return c, hot, late


def build(nc, x, pT, w_in, w_out, w_ple, w_moe, w_gate, w_route, gains, cols, rows, rel_bias,
          consts, hot, late, y_prompt, y_sample):
    bias_dram = nc.dram_tensor("bias_table", (MAPS, REL), F32, kind="Internal").ap()
    h2_dram = nc.dram_tensor("h2_rows", (TOK, D), F32, kind="Internal").ap()
    y_dram = nc.dram_tensor("moe_rows", (MOE_TILES * P, D), F32, kind="Internal").ap()

    ctx = ExitStack()
    with ctx:
        base = 16512
        sizes = dict(W=WS * 8192, RAW=RS * 4096, A=49152, R1=12288, R2=12288, R3=12288, R4=12288,
                     TMP=8192, X=7168, S=9568)
        at, o = {}, base
        for k, v in sizes.items():
            at[k] = o
            o += v

        def sb(name, shape, dt, region, off=0):
            return nc.alloc_sbuf_tensor_at(name, shape, dt, offset=at[region] + off)

        small = [0]

        def sm(name, n, dt=F32):
            t = sb(name, [P, n], dt, "S", small[0])
            small[0] += (4 * n + 31) // 32 * 32
            assert small[0] <= sizes["S"], small[0]
            return t

        W = sb("w_split", [P, WS, 2, 2, N], F32R, "W")
        RAW = sb("w_raw", [P, RS, 2, N], F32, "RAW")
        hT = sb("h_T", [P, 2, KD, TOK], F32R, "A")
        xt = [sb(f"x_tile{i}", [P, D], F32, r, 4096 * o_) for i, (r, o_) in enumerate(
            (("TMP", 0), ("TMP", 1), ("R2", 0), ("R2", 1), ("R2", 2), ("R4", 1)))]
        tok_tmp = [sb(f"tok_tmp{i}", [P, N], F32, "TMP", 2048 * i) for i in range(2)]
        sq_tmp = sb("sq_tmp", [P, N], F32, "TMP", 4096)
        u_tok = sb("u_tok", [P, TILES, N], F32, "R1")
        uT = sb("u_T", [P, 4, TOK], F32, "R2")
        convT = sb("conv_T", [P, 4, TOK], F32, "R1")
        qT = sb("q_T", [P, HEADS, TOK], F32, "R3")
        kT = sb("k_T", [P, HEADS, TOK], F32, "R2")
        v = sb("v_tok", [P, TILES, N], F32, "R4")
        zeros = sb("zeros", [P, N], F32, "X")
        junk = sb("junk", [P, D], F32, "X", 3072)
        hot_sb = sb("hot_sb", [BUCKETS, REL], F32, "R3")
        bias_sb = sb("bias_sb", [MAPS, REL], F32, "R3", 4096)
        o_tok = sb("o_tok", [P, TILES, N], F32, "A")
        mixA = [sb(f"mix_att{i}", [P, HEADS, TOK], F32R, "A", 12288 * (1 + i)) for i in range(2)]
        toep = [sb("toep0", [P, 2, GW], F32, "X"), sb("toep1", [P, 2, GW], F32, "A", 36864)]
        aT = [sb(f"a_T{i}", [P, N], F32, "A", 44032 + 2048 * i) for i in range(2)]
        ojunk = sb("o_junk", [P, VD], F32, "A", 48128)
        s_sb = [[sb(f"s{i}_{m}", [P, N], F32, "TMP", 4096 * i + 2048 * m) for m in range(2)]
                for i in range(2)]
        mixC = [sb("mix_conv0", [P, 4, TOK], F32R, "R2"), sb("mix_conv1", [P, 4, TOK], F32R, "R3")]
        x2 = [sb(f"x2_{i}", [P, D], F32, "R4" if i < 3 else "R1", 4096 * (i % 3)) for i in range(TILES)]
        h2 = [sb(f"h2_{i}", [P, D], F32, "A", 4096 * (i % 3) + (0 if i < 3 else 36864))
              for i in range(TILES)]
        xr = [sb(f"x_again{i}", [P, D], F32, "TMP", 4096 * i) for i in range(2)]
        h2T = sb("h2_T", [P, KD, P], F32, "X")
        cl = sb("late_sb", [P, L_N], F32, "X", 4096)
        src_u = sb("slot_token", [P, MOE_TILES], U32, "X", 4864)
        rank_hot = sb("rank_hot", [P, 2 * TILES, P], F32, "A")
        now_u = sb("tile_tokens", [P, 1], U32, "X", 6400)
        ge_sl = sb("slot_ge", [P, 2 * TILES, MOE_TILES + 1], F32, "X", 4992)
        tile_hot = sb("tile_hot", [P, 2 * TILES, MOE_TILES], F32, "X")
        pTs = [sb(f"p_T{i}", [P, 2, TOK], F32R, "R2", 6144 * i) for i in range(2)]
        p_raw = sb("p_raw", [P, 2, TOK], F32, "R3")
        ejunk = sb("e_junk", [P, D], F32, "A", 45056)
        ple = [sb(f"ple{i}", [P, D], F32, "A", 12288 + 4096 * i) for i in range(TILES)]
        more = [sb(f"w_raw_more{i}", [P, 2, N], F32, "A", o_)
                for i, o_ in enumerate((8192, 36864, 40960, 4096))]
        xg = sb("moe_x", [P, D], F32, "R3", 8192)
        xgT = [sb(f"moe_xT{i}", [P, KD, P], F32R, "R2", 4096 * (1 + i)) for i in range(2)]
        actT = [sb(f"moe_actT{i}", [P, 2, P], F32R, "R3", 1024 * i) for i in range(2)]
        sg = sb("moe_silu", [P, DE], F32, "R3", 2048)
        act_t = sb("moe_act", [P, DE], F32, "R3", 3072)
        yb = sb("moe_y", [P, 2, N], F32, "R3", 4096)
        ga = [sb("pick0_0", [P, D], F32, "A", 0), sb("pick0_1", [P, D], F32, "A", 36864)]
        gb = [sb("pick1_0", [P, D], F32, "A", 4096), sb("pick1_1", [P, D], F32, "A", 40960)]
        x3T = [[sb(f"x3T{i}_{j}", [P, KD, P], F32R, "R2" if 2 * i + j < 3 else "R3",
                   4096 * ((2 * i + j) % 3)) for j in range(2)] for i in range(2)]
        sig = sb("sig", [P, D], F32, "R3", 4096)
        outb = sb("out_tile", [P, D], F32, "R3", 8192)
        roff = [0]

        def rt(name, *shape):
            n = int(np.prod(shape))
            t = sb(name, [P, *shape], F32, "TMP", roff[0])
            roff[0] += (4 * n + 31) // 32 * 32
            assert roff[0] <= 8192
            return t

        r_lg = rt("r_lg", TILES, ROUTES)
        r_gm = rt("r_gm", TILES)
        r_ge = rt("r_ge", TILES, G)
        r_gs = rt("r_gs", TILES)
        r_oh = rt("r_oh", TILES, G)
        r_sc = rt("r_sc", TILES, G)
        r_sel = rt("r_sel", TILES, EPG)
        r_m1, r_m2 = rt("r_m1", TILES), rt("r_m2", TILES)
        r_o1, r_o2 = rt("r_o1", TILES, EPG), rt("r_o2", TILES, EPG)
        r_e2 = rt("r_e2", TILES)
        r_O = [rt(f"r_O{j}", TILES, G, EPG) for j in range(2)]
        r_M = rt("r_M", TILES + 1, E)
        r_C = rt("r_C", TILES, E)
        r_big = rt("r_big", TILES, E)
        r_slot = rt("r_slot", TILES, E)
        r_t = rt("r_t", TILES, E)
        r_cnt = rt("r_cnt", E)
        r_ov = rt("r_ov", E, 6)
        r_b = rt("r_b", E)
        r_inc = rt("r_inc", E)
        r_base = rt("r_base", E)
        r_et = rt("r_et", OVER_TILES, E)
        r_ef = rt("r_ef", OVER_TILES + 1)
        r_sl, r_tl, r_rk = (rt(n, 2 * TILES) for n in ("r_sl", "r_tl", "r_rk"))

        cst = sm("cst", C_N)
        gain = sb("gain_row", [P, D], F32, "S", small[0])
        pad = [sb(f"q_pad{i}", [P, 2, P], F32, "S", small[0] + 1024 * i) for i in range(2)]
        lamv = sb("lam_rows", [P, 4 * HD], F32, "R4")
        small[0] += 4096
        colv = sm("colv", 16)
        bias_row = sm("bias_row", ROUTES)
        relb = sm("relb", MAPS)
        wr = sb("w_route_sb", [P, KD, ROUTES], F32, "S", small[0])
        small[0] += 4 * KD * ROUTES
        eps = sm("eps_t", 1)
        lam = sm("lam_t", 8)
        gs = sm("gs_t", 1)
        tabs = sm("table_out", 6)
        x_ssq, x_std = sm("x_ssq", TILES), sm("x_std", TILES)
        qk_ss = sm("qk_ss", 96)
        mn, Z, rz = (sm(n, 48) for n in ("mn", "Z", "rz"))
        ratio, o_ssq = sm("ratio", 24), sm("o_ssq", 24)
        x2_ssq = sm("x2_ssq", TILES)
        e_ssq = sm("e_ssq", TILES)
        slot_u = sm("slot_u", 2 * TILES, U32)
        wgt = sm("wgt", 2 * TILES)
        etab = sm("etab", MOE_TILES, I32)
        last_tile = sm("last_tile", 1, I32)

        bank = [ctx.enter_context(nc.psum_tensor(f"bank{i}", [P, N], F32)) for i in range(8)]

        def sem(name):
            return ctx.enter_context(nc.semaphore(name))

        c_ld = sem("consts_loaded")
        gain_ld = sem("gain_loaded")
        raw_ld = [sem(f"raw_loaded{i}") for i in range(RS)]
        more_ld = [sem(f"raw_more_loaded{i}") for i in range(4)]
        hi_done, lo_done = sem("w_hi_done"), sem("w_lo_done")
        w_used = sem("w_unit_used")
        x_ld = [sem(f"x_loaded{i}") for i in range(TILES)]
        id_ld = sem("identity_loaded")
        a_x, d_x = sem("act_x_stats"), sem("dve_x_normed")
        pe_t, t_hi = sem("pe_transposed"), sem("act_hT_hi")
        t_free = [sem(f"t_bank_free{i}") for i in range(4)]
        pe_acc = sem("pe_projected")
        acc_free = [sem(f"acc_bank_free{i}") for i in range(3)]
        dch = sem("dve_steps")
        ach = sem("act_steps")
        gch = sem("pool_steps")
        a_sq, d_ss, a_sd = sem("act_qk_square"), sem("dve_qk_sum"), sem("act_qk_std")
        a_lam = sem("act_lambda_exp")
        z_done, z_st = sem("zeros_set"), sem("slots_zeroed")
        pe_b, a_b, b_st = sem("pe_bias"), sem("act_bias"), sem("bias_stored")
        toep_ld = [sem(f"toep_loaded{i}") for i in range(2)]
        p_pad, pe_s, d_s, a_e, d_a = (sem(n) for n in (
            "pool_q_padded", "pe_scores", "dve_scores", "act_exp", "dve_a"))
        pe_at, a_at, pe_o, a_o = (sem(n) for n in (
            "pe_aT", "act_aT", "pe_o", "act_o"))
        a_os, d_on, pe_ot, a_mix, d_mix, a_mixc, d_mixc = (sem(n) for n in (
            "act_o_std", "dve_o_normed", "pe_oT", "act_mix_hi", "dve_mix_lo", "act_conv_hi",
            "dve_conv_lo"))
        xr_ld = [sem(f"x_again{i}") for i in range(2)]
        pe_wo, d_x2, a_x2, d_h2, pe_h2, a_h2, pe_r = (sem(n) for n in (
            "pe_out_proj", "dve_x2", "act_x2_stats", "dve_h2", "pe_h2T", "act_h2T", "pe_routes"))
        d_lg, a_g, a_e2, d_m, pe_rk, d_route = (sem(n) for n in (
            "dve_logits", "act_group_exp", "act_second_exp", "dve_masks", "pe_ranks", "dve_routed"))
        p_ld, a_p, d_p, pe_ple, a_ple, g_ple = (sem(n) for n in (
            "p_loaded", "act_p_hi", "dve_p_lo", "pe_ple", "act_ple", "pool_ple"))
        h_st, late_ld, d_hot, pe_tab, d_tab, g_now, g_go = (sem(n) for n in (
            "h2_stored", "late_loaded", "dve_one_hots", "pe_slot_table", "dve_slot_table", "pool_tile_tokens", "pool_tokens_seen"))
        xg_ld, pe_xt, a_xt, d_xt = (sem(n) for n in (
            "moe_x_loaded", "pe_moe_xT", "act_moe_xT_hi", "dve_moe_xT_lo"))
        pe_gu, a_si, d_act, pe_aT2, a_aT2, d_aT2, pe_y, a_y, d_y = (sem(n) for n in (
            "pe_gate_up", "act_silu", "dve_act", "pe_actT", "act_actT_hi", "dve_actT_lo",
            "pe_down", "act_y", "dve_y"))
        y_st = [sem(f"y_stored{i}") for i in range(2)]
        pk_ld = [sem(f"picked{i}") for i in range(2)]
        d_x3, pe_x3, a_x3, d_x3t, pe_g, a_g2, d_out = (sem(n) for n in (
            "dve_x3", "pe_x3T", "act_x3_hi", "dve_x3_lo", "pe_gate", "act_sigmoid", "dve_out",
            ))
        o_st = [sem(f"out_stored{i}") for i in range(2)]

        ident = cst[:, C_ID:C_ID + P]

        def tk(i):
            return slice(i * P, (i + 1) * P)

        def f(t):
            return t.bitcast(F32)

        def slot_free(eng, u):
            v0 = u - WS
            if v0 < 0:
                return
            if v0 < OUT0:
                b, j = divmod(v0, 4)
                if j < 3:
                    eng.wait_ge(w_used, 3 * b + j + 1)
                else:
                    eng.wait_ge(pe_acc, TILES * (b + 1))
            else:
                out_unit_used(eng, v0 - OUT0)

        def out_unit_used(eng, j):
            if j % 4 < 3:
                eng.wait_ge(w_used, 18 + 3 * (j // 4) + j % 4 + 1)
            else:
                eng.wait_ge(pe_wo, 2 * (TILES - 1) + 1 + j // 4)

        UP1, DOWN0 = MOE0 + 4, MOE0 + 8
        DOWN_LAST, GATE0 = MOE0 + 10, MOE0 + 12

        def up_used(eng, t, j):
            if j < 3:
                eng.wait_ge(w_used, t * 3 + (24 + j + 1))
            else:
                eng.wait_ge(pe_gu, t + 1)

        def down_used(eng, t, j):
            eng.wait_ge(pe_y, t * 2 + (j + 1))

        def moe_hi(u, t, slot):
            src, loaded, n = raw(u)
            nc.scalar.wait_ge(loaded, t * 16 + 16 * n)
            nc.scalar.activation(W[:, slot, 0], src, ACT.Copy).then_inc(hi_done, 1)

        MORE0 = MOE0 + 6

        def raw(u):
            if MORE0 <= u < MORE0 + 4:
                return more[u - MORE0][:], more_ld[u - MORE0], 1
            r = u if u < MORE0 else u - 4
            return RAW[:, r % RS], raw_ld[r % RS], r // RS + 1

        def split_hi(u):
            src, loaded, n = raw(u)
            nc.scalar.wait_ge(loaded, 16 * n)
            nc.scalar.activation(W[:, u % WS, 0], src, ACT.Copy).then_inc(hi_done, 1)

        def split_lo(u):
            nc.vector.wait_ge(hi_done, u + 1)
            nc.vector.tensor_tensor(W[:, u % WS, 1], raw(u)[0], f(W[:, u % WS, 0]),
                                    ALU.subtract).then_inc(lo_done, 1)

        def three(out, hi, lo, whi, wlo, first, last):
            nc.tensor.matmul(out, hi, whi, start=first, stop=False)
            nc.tensor.matmul(out, lo, whi, start=False, stop=False)
            return nc.tensor.matmul(out, hi, wlo, start=False, stop=last)

        def t_ready(eng, m):
            eng.wait_ge(t_free[m % 4], m // 4 + 1)

        TJ = {X_B: 12, GATE_B: 18, Q_B: 24, K_B: 30}
        def keys(i):
            return (0, SEQS[0]) if i < PROMPT_TILES else (SEQS[0], SEQS[1])

        ITEMS = [(h, i) for h in range(HEADS) for i in range(TILES)]
        NI = len(ITEMS)
        LATE_UNITS = {2 + j: OUT0 + 4 + j for j in range(4)}

        block = ctx.enter_context(nc.Block())

        @block.sync
        def _(sp):
            def unit(src, u):
                dst, loaded, _ = raw(u)
                if RS <= u < MORE0:
                    sp.wait_ge(lo_done, u - RS + 1)
                elif u >= MORE0 + 4:
                    sp.wait_ge(lo_done, u - 4 - RS + 1)
                sp.dma_start(dst, src).then_inc(loaded, 16)

            def x_tile(i):
                sp.dma_start(xt[i][:], x[tk(i)]).then_inc(x_ld[i], 16)

            def toeplitz(h):
                if h == 1:
                    sp.wait_ge(pe_acc, 36)
                elif h == 0:
                    sp.wait_ge(z_st, 16 * (OVER_TILES - 1))
                    for half in range(2):
                        sp.wait_ge(y_st[half], 16)
                    sp.wait_ge(ach, 6)
                else:
                    sp.wait_ge(d_s, 2 * TILES * (h - 1))
                src = bass.AP(bias_dram.tensor, 2 * h * REL + 1,
                              [[1, P], [REL, 2], [1, GW]])
                sp.dma_start(toep[h % 2][:], src).then_inc(toep_ld[h % 2], 16)

            x_tile(0)
            sp.dma_start(gain[:], gains[0]).then_inc(gain_ld, 16)
            unit(w_in[0], 0)
            x_tile(1)
            for i in range(1, 4):
                unit(w_in[i], i)
                x_tile(i + 1)
            x_tile(TILES - 1)
            for u in range(4, OUT0 + 4):
                unit(w_in[u] if u < OUT0 else w_out[u - OUT0], u)
                if u == 8:
                    sp.wait_ge(a_b, 2)
                    sp.dma_start(bias_dram, bias_sb[:]).then_inc(b_st, 16)
                if u == 20:
                    sp.wait_ge(b_st, 16)
                    toeplitz(0)
            toeplitz(1)
            for u in range(OUT0 + 4, PLE0):
                unit(w_out[u - OUT0], u)
            toeplitz(2)
            toeplitz(3)
            sp.wait_ge(pe_s, 2 * NI)
            sp.dma_start(gain[:], gains[1]).then_inc(gain_ld, 16)
            sp.wait_ge(pe_at, NI)
            sp.dma_start(cl[:], late).then_inc(late_ld, 16)

            def store_h2(i):
                sp.wait_ge(d_h2, 2 * i + 2)
                sp.dma_start(h2_dram[tk(i)], h2[i][:]).then_inc(h_st, 16)

            for i in range(TILES):
                if i >= 3:
                    store_h2(i - 3)
                if i >= 2:
                    sp.wait_ge(d_x2, 2 * (i - 2) + 2)
                if i == 2:
                    for u in range(PLE0, MOE0):
                        unit(w_ple[u - PLE0], u)
                sp.dma_start(xr[i % 2][:], x[tk(i)]).then_inc(xr_ld[i % 2], 16)
            for j in range(4):
                unit(w_moe[0, j], MOE0 + j)
            for i in range(TILES - 3, TILES - 1):
                store_h2(i)
            sp.wait_ge(pe_wo, 2 * TILES)
            sp.dma_start(p_raw[:], pT).then_inc(p_ld, 16)
            store_h2(TILES - 1)
            sp.dma_start(gain[:], gains[2]).then_inc(gain_ld, 16)
            for j in range(4):
                if j == 2:
                    sp.wait_ge(h_st, 16 * TILES)
                    sp.wait_ge(pe_h2, 2 * (TILES - 1))
                unit(w_moe[1, j], UP1 + j)
            unit(w_moe[0, 4], DOWN0)
            sp.wait_ge(pe_tab, 1)
            unit(w_moe[0, 5], DOWN0 + 1)
            for j in range(4):
                unit(w_moe[2, j], UP1 + 6 + j)
            for j in range(2):
                unit(w_moe[1, 4 + j], DOWN0 + 6 + j)

            def moe_unit(src, u, t):
                dst, loaded, _ = raw(u)
                sp.wait_ge(lo_done, t * 6 + (u - RS + 1))
                sp.dma_start(dst, src).then_inc(loaded, 16)

            def of_expert(t, j):
                ex = sp.value_load(etab[0:1, bass.ds(t, 1)], min_val=0, max_val=E - 1)
                return w_moe[bass.ds(ex, 1), j[0]:j[1]].rearrange("a j p k n -> (a j) p k n")

            sp.wait_ge(d_route, 1)
            m = sp.value_load(last_tile[0:1, 0:1], min_val=E - 2, max_val=MOE_TILES - 2)
            with sp.Fori(1, m) as t:
                up = of_expert(t + 2, (0, 4))
                for j in range(4):
                    moe_unit(up[j], UP1 + 6 + j, t)
                down = of_expert(t + 1, (4, 6))
                for j in range(2):
                    moe_unit(down[j], DOWN0 + 6 + j, t)
            down = of_expert(m + 1, (4, 6))
            for j in range(2):
                moe_unit(down[j], DOWN_LAST + j, m)
            for g in range(FIN_UNITS):
                moe_unit(w_gate[g], GATE0 + g, m)
            for i in range(TILES):
                dst = y_prompt[tk(i)] if i < PROMPT_TILES else y_sample[tk(i - PROMPT_TILES)]
                for half in range(2):
                    c = slice(half * N, (half + 1) * N)
                    sp.wait_ge(d_out, 2 * i + half + 1)
                    sp.dma_start(dst[:, c], outb[:, c]).then_inc(o_st[half], 16)
            for half in range(2):
                sp.wait_ge(o_st[half], 16 * TILES)

        @block.gpsimd
        def _(pool):
            pool.memset(zeros[:], 0.0).then_inc(z_done, 1)
            pool.wait_ge(z_done, 1)
            for t in range(OVER_TILES):
                pool.wait_ge(pe_acc, TILES + 1 + t)
                rows_ = y_dram[tk(E + t)]
                if t < OVER_TILES - 1:
                    pool.dma_start(rows_.rearrange("p (n z) -> p n z", z=N),
                                   zeros[:].unsqueeze(1).broadcast_to([P, 2, N])).then_inc(z_st, 16)
                else:
                    for half in range(2):
                        pool.dma_start(rows_[:, half * N:(half + 1) * N], zeros[:]).then_inc(y_st[half], 16)

            pool.wait_ge(d_x, 2 * TILES)
            for i in range(2):
                pool.memset(pad[i][HD:P, 0, :], 0.0).then_inc(gch, 1)
                pool.memset(pad[i][0:HD, 1, :], 0.0).then_inc(gch, 1)
            pool.wait_ge(gch, 4)
            t_ready(pool, TJ[Q_B] + 5)
            t_ready(pool, TJ[Q_B] + 4)
            t_ready(pool, TJ[Q_B] + 3)
            t_ready(pool, TJ[Q_B] + 2)
            for w, (h, i) in enumerate(ITEMS):
                if w >= 2:
                    pool.wait_ge(pe_s, 2 * (w - 1))
                for m in range(2):
                    r = slice(m * HD, (m + 1) * HD)
                    pool.tensor_copy(pad[w % 2][r, m, :], qT[r, h, tk(i)]).then_inc(p_pad, 1)

            def gather_x(t):
                pool.tensor_copy(now_u[:], src_u[:, bass.ds(t, 1)]).then_inc(g_now, 1)
                pool.wait_ge(g_now, t + 1)
                pool.sem_inc(g_go, 1)
                pool.indirect_dma_start(
                    xg[:], None, h2_dram,
                    bass.IndirectOffsetOnAxis(ap=now_u[:], axis=0)).then_inc(xg_ld, 16)

            def ple_gain(i):
                pool.wait_ge(a_ple, 3 * i + 3)
                pool.tensor_tensor(ple[i][:], ple[i][:], gain[:], ALU.mult).then_inc(g_ple, 1)

            def store_y(t, back, halves=(0, 1)):
                for half in halves:
                    pool.wait_ge((a_y, d_y)[half], t + (2 - back))
                    pool.dma_start(y_dram[bass.ds(t * P - back * P, P), half * N:(half + 1) * N],
                                   yb[:, half]).then_inc(y_st[half], 16)

            pool.wait_ge(h_st, 16 * TILES)
            pool.wait_ge(d_tab, 1)
            gather_x(0)
            pool.wait_ge(gain_ld, 48)
            ple_gain(0)
            pool.wait_ge(pe_xt, 2)
            gather_x(1)
            for i in range(1, TILES):
                ple_gain(i)
            pool.wait_ge(z_st, 16 * (OVER_TILES - 1))
            for half in range(2):
                pool.wait_ge(y_st[half], 16)
            m = pool.value_load(last_tile[0:1, 0:1], min_val=E - 2, max_val=MOE_TILES - 2)
            pool.wait_ge(pe_xt, 4)
            gather_x(2)
            with pool.Fori(1, m) as t:
                store_y(t, 1, (0,))
                pool.wait_ge(pe_xt, t * 2 + 4)
                gather_x(t + 2)
                store_y(t, 1, (1,))
            store_y(m, 1)
            store_y(m, 0)
            store_y(m + 1, 0)
            for half in range(2):
                pool.wait_ge(y_st[half], m * 16 + 48)
            pool.sem_inc(g_go, 1)

            for i in range(TILES):
                if i >= 2:
                    pool.wait_ge(d_x3, 2 * (i - 1))
                for j, buf in ((0, ga), (1, gb)):
                    c = j * TILES + i
                    pool.indirect_dma_start(
                        buf[i % 2][:], None, y_dram,
                        bass.IndirectOffsetOnAxis(ap=slot_u[:, c:c + 1], axis=0)
                    ).then_inc(pk_ld[i % 2], 16)

        @block.scalar
        def _(act):
            act.dma_start(cst[:], consts).then_inc(id_ld, 16)
            act.dma_start(lamv[:], rows[:, 0:4 * HD]).then_inc(c_ld, 16)
            act.dma_start(colv[:, 0:15], cols).then_inc(c_ld, 16)
            act.dma_start(bias_row[:], rows[:, 4 * HD:4 * HD + ROUTES]).then_inc(c_ld, 16)
            act.dma_start(relb[0:BUCKETS, :], rel_bias).then_inc(c_ld, 16)
            act.dma_start(hot_sb[:], hot).then_inc(c_ld, 16)
            act.dma_start(wr[:], w_route).then_inc(c_ld, 16)

            def x_stats(i):
                act.wait_ge(x_ld[i], 16)
                if i == 0:
                    act.wait_ge(dch, 1)
                else:
                    act.wait_ge(ach, i)
                act.activation(junk[:], xt[i][:], ACT.Square,
                               accum_out=x_ssq[:, i:i + 1]).then_inc(ach, 1)
                act.wait_ge(ach, i + 1)
                act.activation(x_std[:, i:i + 1], x_ssq[:, i:i + 1], ACT.Sqrt, bias=eps[:],
                               scale=1.0 / D).then_inc(a_x, 1)

            def hT_hi(i):
                for half in range(2):
                    m = 2 * i + half
                    act.wait_ge(pe_t, m + 1)
                    act.activation(hT[:, 0, 4 * half:4 * half + 4, tk(i)],
                                   bank[3 + m % 4][:].rearrange("p (k t) -> p k t", k=4),
                                   ACT.Copy).then_inc(t_hi, 1)

            def table(func, c):
                act.activation(tabs[:, c:c + 1], eps[:], func)

            act.wait_ge(dch, 1)
            table(ACT.Sqrt, 0)
            x_stats(0)
            split_hi(0)
            x_stats(1)
            hT_hi(0)
            for u in range(1, 4):
                split_hi(u)
            hT_hi(1)
            x_stats(2)

            def exps(w):
                nk = keys(ITEMS[w][1])[1]
                for m in range(2):
                    act.wait_ge(d_s, 2 * w + m + 1)
                    s = s_sb[w % 2][m][:, 0:nk]
                    act.activation(s, s, ACT.Exp, bias=mn[:, 2 * w + m:2 * w + m + 1], scale=-1.0,
                                   accum_out=Z[:, 2 * w + m:2 * w + m + 1]).then_inc(a_e, 1)

            def conv_hi(i):
                act.wait_ge(pe_s, 2 * NI)
                act.activation(mixC[0][:, :, tk(i)], convT[:, :, tk(i)], ACT.Copy).then_inc(a_mixc, 1)

            def next_unit(b, i):
                u = 4 * (b + 1) + i
                if i < 4:
                    slot_free(act, u)
                    split_hi(u)

            for b in range(6):
                for i in range(TILES):
                    n = TILES * b + i
                    if b == CONV_B:
                        if i + 3 < TILES:
                            x_stats(i + 3)
                        if i + 2 < TILES:
                            hT_hi(i + 2)
                        act.wait_ge(pe_acc, n + 1)
                        act.activation(u_tok[:, i], bank[n % 3][:], ACT.Copy).then_inc(acc_free[n % 3], 1)
                    elif b == X_B:
                        m = TJ[b] + i
                        act.wait_ge(pe_t, m + 1)
                        act.activation(uT[:, :, tk(i)], bank[3 + m % 4][:].rearrange(
                            "p (k t) -> p k t", k=4), ACT.Copy).then_inc(t_free[m % 4], 1)
                    elif b == GATE_B:
                        act.wait_ge(pe_acc, n + 1)
                        if i >= 2:
                            act.wait_ge(pe_t, TJ[b] + i - 1)
                        act.activation(tok_tmp[i % 2][:], bank[n % 3][:],
                                       ACT.Copy).then_inc(acc_free[n % 3], 1)
                    elif b in (Q_B, K_B):
                        r = n - TILES * Q_B
                        act.wait_ge(pe_acc, n + 1)
                        if r >= 1:
                            act.wait_ge(d_ss, r)
                        act.activation(sq_tmp[:], bank[n % 3][:], ACT.Square).then_inc(a_sq, 1)
                        act.wait_ge(d_ss, r + 1)
                        act.activation(qk_ss[:, 8 * r:8 * r + 8], qk_ss[:, 8 * r:8 * r + 8], ACT.Sqrt,
                                       bias=eps[:], scale=1.0 / HD).then_inc(a_sd, 1)
                    else:
                        if i == 0:
                            table(ACT.Exp, 1)
                        act.wait_ge(pe_acc, n + 1)
                        act.activation(v[:, i], bank[n % 3][:], ACT.Copy).then_inc(acc_free[n % 3], 1)
                        if i == 3:
                            exps(0)
                    next_unit(b, i)
                if b == CONV_B:
                    for half in range(2):
                        act.wait_ge(pe_b, half + 1)
                        act.activation(bias_sb[:, half * N:(half + 1) * N], bank[7][0:MAPS],
                                       ACT.Copy, scale=-1.0).then_inc(a_b, 1)
                    act.wait_ge(dch, 3)
                    act.activation(lam[:, 0:2], lam[:, 0:2], ACT.Exp).then_inc(a_lam, 1)

            def evac_aT(w):
                nk = keys(ITEMS[w][1])[1]
                act.wait_ge(pe_at, w + 1)
                if w >= 2:
                    act.wait_ge(pe_o, w - 1)
                act.activation(aT[w % 2][:, 0:nk], bank[(7, 0)[w % 2]][:, 0:nk], ACT.Copy).then_inc(a_at, 1)

            def o_out(w):
                h, i = ITEMS[w]
                o_, z = bank[1 + w % 2][:, 0:VD], rz[:, 2 * w:2 * w + 1]
                act.wait_ge(pe_o, w + 1)
                act.activation(o_tok[:, i, h * VD:(h + 1) * VD], o_, ACT.Copy, scale=z).then_inc(a_o, 1)
                if w >= 1:
                    act.wait_ge(a_o, 2 * w)
                act.activation(ojunk[:], o_, ACT.Square, scale=z,
                               accum_out=o_ssq[:, w:w + 1]).then_inc(a_o, 1)

            exps(1)
            for w in range(2, NI + 3):
                if w < NI + 2:
                    evac_aT(w - 2)
                if w < NI:
                    exps(w)
                if NI <= w < NI + 2:
                    conv_hi(w - NI)
                if w == NI + 1:
                    table(ACT.Sqrt, 2)
                if w >= 3:
                    o_out(w - 3)
                if w in LATE_UNITS:
                    slot_free(act, LATE_UNITS[w])
                    split_hi(LATE_UNITS[w])

            act.wait_ge(a_o, 2 * NI)
            act.activation(o_ssq[:], o_ssq[:], ACT.Sqrt, bias=eps[:], scale=1.0 / VD).then_inc(a_os, 1)
            for i in range(TILES):
                act.wait_ge(pe_ot, i + 1)
                act.activation(mixA[0][:, :, tk(i)], bank[(7, 0)[i % 2]][:].rearrange(
                    "p (k t) -> p k t", k=4), ACT.Copy, scale=gs[:]).then_inc(a_mix, 1)
                if i >= 2:
                    conv_hi(i)

            def x2_stats(i):
                act.wait_ge(d_x2, 2 * i + 2)
                act.activation(h2[i][:], x2[i][:], ACT.Square,
                               accum_out=x2_ssq[:, i:i + 1]).then_inc(a_x2, 1)
                act.wait_ge(a_x2, 2 * i + 1)
                act.activation(x2_ssq[:, i:i + 1], x2_ssq[:, i:i + 1], ACT.Sqrt, bias=eps[:],
                               scale=1.0 / D).then_inc(a_x2, 1)

            def h2T_out(i):
                for half in range(2):
                    act.wait_ge(pe_h2, 2 * i + half + 1)
                    if half == 0 and i >= 1:
                        act.wait_ge(pe_r, i)
                    act.activation(h2T[:, 4 * half:4 * half + 4], bank[1 + half][:].rearrange(
                        "p (k t) -> p k t", k=4), ACT.Copy).then_inc(a_h2, 1)

            for i in range(TILES - 1):
                x2_stats(i)
                if i < TILES - 2:
                    h2T_out(i)
            for u in range(PLE0, MOE0):
                slot_free(act, u)
                split_hi(u)
            h2T_out(TILES - 2)
            x2_stats(TILES - 1)
            act.wait_ge(p_ld, 16)
            act.activation(pTs[0][:], p_raw[:], ACT.Copy).then_inc(a_p, 1)
            h2T_out(TILES - 1)

            table(ACT.Exp, 3)
            act.wait_ge(d_lg, 1)
            act.activation(r_ge[:], r_ge[:], ACT.Exp).then_inc(a_g, 1)
            act.wait_ge(d_lg, 2)
            act.activation(r_e2[:], r_e2[:], ACT.Exp).then_inc(a_e2, 1)

            act.wait_ge(h_st, 16 * TILES)
            for i in range(TILES):
                for half in range(2):
                    act.wait_ge(pe_ple, 2 * i + half + 1)
                    act.activation(ple[i][:, half * N:(half + 1) * N], bank[3 + 2 * (i % 2) + half][:],
                                   ACT.Copy).then_inc(a_ple, 1)
                act.wait_ge(a_ple, 3 * i + 2)
                act.activation(ejunk[:], ple[i][:], ACT.Square,
                               accum_out=e_ssq[:, i:i + 1]).then_inc(a_ple, 1)
                act.wait_ge(a_ple, 3 * i + 3)
                act.activation(e_ssq[:, i:i + 1], e_ssq[:, i:i + 1], ACT.Sqrt, bias=eps[:],
                               scale=1.0 / D).then_inc(ach, 1)
                if i < 4:
                    slot_free(act, MOE0 + i)
                    split_hi(MOE0 + i)

            act.wait_ge(d_route, 1)
            m = act.value_load(last_tile[0:1, 0:1], min_val=E - 2, max_val=MOE_TILES - 2)

            def xT_hi(t, half):
                act.wait_ge(pe_xt, t * 2 + (half + 1))
                act.activation(xgT[0][:, 4 * half:4 * half + 4], bank[1 + half][:].rearrange(
                    "p (k t) -> p k t", k=4), ACT.Copy).then_inc(a_xt, 1)

            def silu(t):
                act.wait_ge(pe_gu, t + 1)
                act.activation(sg[:], bank[0][:, 0:DE], ACT.Silu).then_inc(a_si, 1)

            def actT_hi(t):
                act.wait_ge(pe_aT2, t + 1)
                act.activation(actT[0][:], bank[3][:, 0:DE].rearrange("p (k t) -> p k t", k=2),
                               ACT.Copy).then_inc(a_aT2, 1)

            def y_left(t):
                act.wait_ge(pe_y, t * 2 + 1)
                act.wait_ge(y_st[0], t * 16 + 16)
                act.activation(yb[:, 0], bank[4][:], ACT.Copy).then_inc(a_y, 1)

            def up_hi(t, j, of):
                up_used(act, t + 1 if of == 2 else 0, j)
                moe_hi(UP1 + j if of == 1 else UP1 + 6 + j, t, 2 + j)

            act.sem_inc(a_y, 1)
            xT_hi(0, 0)
            xT_hi(0, 1)
            table(ACT.Silu, 4)
            for j in range(3):
                up_hi(0, j, 1)
            silu(0)
            xT_hi(1, 0)
            xT_hi(1, 1)
            up_hi(0, 3, 1)
            for j in range(2):
                moe_hi(DOWN0 + j, 0, 6 + j)
            with act.Fori(0, m) as t:
                up_hi(t, 0, 2)
                actT_hi(t)
                up_hi(t, 1, 2)
                up_hi(t, 2, 2)
                silu(t + 1)
                xT_hi(t + 2, 0)
                xT_hi(t + 2, 1)
                up_hi(t, 3, 2)
                y_left(t)
                for j in range(2):
                    down_used(act, t, j)
                    moe_hi(DOWN0 + 6 + j, t, 6 + j)
            actT_hi(m)
            silu(m + 1)
            act.wait_ge(pe_ple, 2 * TILES)
            for j in range(2):
                moe_hi(DOWN_LAST + j, m, j)
            y_left(m)
            actT_hi(m + 1)

            for g in range(FIN_UNITS):
                if g == 1:
                    y_left(m + 1)
                if g < 4:
                    up_used(act, m + 1, g)
                else:
                    down_used(act, m + (0 if g < 6 else 1), g % 2)
                moe_hi(GATE0 + g, m, (g + 2) % WS)

            def x3T_hi(i):
                for half in range(2):
                    act.wait_ge(pe_x3, 2 * i + half + 1)
                    act.activation(x3T[i % 2][0][:, 4 * half:4 * half + 4], bank[6 + half][:].rearrange(
                        "p (k t) -> p k t", k=4), ACT.Copy).then_inc(a_x3, 1)

            table(ACT.Sigmoid, 5)
            x3T_hi(0)
            for i in range(TILES):
                if i + 1 < TILES:
                    x3T_hi(i + 1)
                for half in range(2):
                    act.wait_ge(pe_g, 2 * i + half + 1)
                    if i >= 1:
                        act.wait_ge(d_out, 2 * (i - 1) + half + 1)
                    act.activation(sig[:, half * N:(half + 1) * N], bank[2 * (i % 2) + half][:],
                                   ACT.Sigmoid).then_inc(a_g2, 1)

        @block.vector
        def _(dve):
            steps = [0]

            def link(ins):
                steps[0] += 1
                ins.then_inc(dch, 1)
                dve.wait_ge(dch, steps[0])

            link(dve.memset(eps[:], EPS))

            def x_norm(i):
                dve.wait_ge(a_x, i + 1)
                if i == 0:
                    dve.wait_ge(gain_ld, 16)
                dve.reciprocal(x_std[:, i:i + 1], x_std[:, i:i + 1]).then_inc(d_x, 1)
                dve.wait_ge(d_x, 2 * i + 1)
                dve.scalar_tensor_tensor(out=xt[i][:], in0=xt[i][:], scalar=x_std[:, i:i + 1],
                                         in1=gain[:], op0=ALU.mult, op1=ALU.mult).then_inc(d_x, 1)

            def hT_lo(i):
                for half in range(2):
                    m = 2 * i + half
                    hi = hT[:, 0, 4 * half:4 * half + 4, tk(i)]
                    dve.wait_ge(t_hi, m + 1)
                    dve.tensor_tensor(hT[:, 1, 4 * half:4 * half + 4, tk(i)],
                                      bank[3 + m % 4][:].rearrange("p (k t) -> p k t", k=4), f(hi),
                                      ALU.subtract).then_inc(t_free[m % 4], 1)

            x_norm(0)
            split_lo(0)
            x_norm(1)
            hT_lo(0)
            for u in range(1, 4):
                split_lo(u)
            hT_lo(1)
            x_norm(2)
            dve.wait_ge(c_ld, 16 * 6)
            for j in range(2):
                ins = dve.tensor_tensor_reduce(lamv[:, 2 * j * HD:(2 * j + 1) * HD],
                                               lamv[:, 2 * j * HD:(2 * j + 1) * HD],
                                               lamv[:, (2 * j + 1) * HD:(2 * j + 2) * HD], 1.0, 0.0,
                                               ALU.mult, ALU.add, lam[:, j:j + 1])
                link(ins)
            link(dve.tensor_scalar(gs[:], colv[:, 2:3], 1.0 - LAMBDA_INIT, None, ALU.mult))

            def tbank(m):
                return bank[3 + m % 4][:].rearrange("p (k t) -> p k t", k=4)

            def gate_mul(i):
                m = TJ[GATE_B] + i
                dve.wait_ge(pe_t, m + 1)
                dve.tensor_tensor(convT[:, :, tk(i)], tbank(m), convT[:, :, tk(i)],
                                  ALU.mult).then_inc(t_free[m % 4], 1)

            def qk_out(b, i):
                m = TJ[b] + i
                dve.wait_ge(pe_t, m + 1)
                if b == Q_B:
                    if i == 0:
                        dve.wait_ge(b_st, 16)
                    ins = dve.tensor_scalar(qT[:, :, tk(i)], tbank(m), colv[:, 0:1], -HD ** -0.5,
                                            ALU.mult, ALU.mult)
                else:
                    ins = dve.tensor_scalar(kT[:, :, tk(i)], tbank(m), colv[:, 1:2], None, ALU.mult)
                ins.then_inc(t_free[m % 4], 1)

            def scores(w):
                h, i = ITEMS[w]
                nk = keys(i)[1]
                qt = i if i < PROMPT_TILES else i - PROMPT_TILES
                c0 = 384 - P * qt
                if i == 0:
                    dve.wait_ge(toep_ld[h % 2], 16 * (h // 2 + 1))
                if w >= 2:
                    dve.wait_ge(pe_at, w - 1)
                for m in range(2):
                    dve.wait_ge(pe_s, 2 * w + m + 1)
                    dve.tensor_tensor_reduce(s_sb[w % 2][m][:, 0:nk],
                                             bank[3 + 2 * (w % 2) + m][:, 0:nk],
                                             toep[h % 2][:, m, c0:c0 + nk], 1.0, 3.0e38,
                                             ALU.add, ALU.min,
                                             mn[:, 2 * w + m:2 * w + m + 1]).then_inc(d_s, 1)

            def combine(w):
                nk = keys(ITEMS[w][1])[1]
                dve.wait_ge(a_e, 2 * w + 2)
                link(dve.reciprocal(rz[:, 2 * w:2 * w + 2], Z[:, 2 * w:2 * w + 2]))
                link(dve.scalar_tensor_tensor(out=ratio[:, w:w + 1], in0=Z[:, 2 * w:2 * w + 1],
                                              scalar=lam[:, 2:3], in1=rz[:, 2 * w + 1:2 * w + 2],
                                              op0=ALU.mult, op1=ALU.mult))
                s0, s1 = (s_sb[w % 2][m][:, 0:nk] for m in range(2))
                dve.scalar_tensor_tensor(out=s0, in0=s1, scalar=ratio[:, w:w + 1], in1=s0,
                                         op0=ALU.mult, op1=ALU.add).then_inc(d_a, 1)

            def conv_lo(i):
                dve.wait_ge(a_mixc, i + 1)
                dve.tensor_tensor(mixC[1][:, :, tk(i)], convT[:, :, tk(i)], f(mixC[0][:, :, tk(i)]),
                                  ALU.subtract).then_inc(d_mixc, 1)

            for b in range(6):
                for i in range(TILES):
                    n = TILES * b + i
                    if b == CONV_B:
                        if i + 3 < TILES:
                            x_norm(i + 3)
                        if i + 2 < TILES:
                            hT_lo(i + 2)
                    elif b == X_B:
                        dve.wait_ge(pe_acc, n + 1)
                        dve.tensor_tensor(u_tok[:, i], bank[n % 3][:], u_tok[:, i],
                                          ALU.mult).then_inc(acc_free[n % 3], 1)
                    elif b in (Q_B, K_B):
                        r = n - TILES * Q_B
                        ss = qk_ss[:, 8 * r:8 * r + 8]
                        if r == 0:
                            gate_mul(TILES - 1)
                        elif i == 0:
                            qk_out(Q_B, TILES - 1)
                        dve.wait_ge(a_sq, r + 1)
                        dve.reduce_sum(ss, sq_tmp[:].rearrange("p (m d) -> p m d", m=MAPS),
                                       AX_X).then_inc(d_ss, 1)
                        if i >= 1:
                            qk_out(b, i - 1)
                        dve.wait_ge(a_sd, r + 1)
                        link(dve.reciprocal(ss, ss))
                        if r >= 2:
                            dve.wait_ge(pe_t, TJ[Q_B] + r - 1)
                        else:
                            dve.wait_ge(pe_t, TJ[GATE_B] + 5 + r)
                        dve.tensor_tensor(tok_tmp[i % 2][:].rearrange("p (m d) -> p m d", m=MAPS),
                                          bank[n % 3][:].rearrange("p (m d) -> p m d", m=MAPS),
                                          ss.unsqueeze(2).broadcast_to([P, MAPS, HD]),
                                          ALU.mult).then_inc(acc_free[n % 3], 1)
                    elif b == GATE_B and i >= 1:
                        gate_mul(i - 1)
                    elif b == V_B and i == 0:
                        qk_out(K_B, TILES - 1)
                    elif b == V_B and i == 3:
                        scores(0)
                    elif b == V_B and i == 4:
                        combine(0)
                    elif b == V_B and i == 5:
                        scores(1)
                    if i < 4:
                        split_lo(4 * (b + 1) + i)
                if b == X_B:
                    for m in range(TJ[X_B] + 2, TJ[X_B] + 6):
                        t_ready(dve, m)
                    for c in range(4):
                        link(dve.tensor_scalar(convT[:, c], uT[:, c], colv[:, 3 + 4 + c:4 + 4 + c],
                                               None, ALU.mult))
                        s0 = 0
                        for s in SEQS:
                            e0 = s0 + s
                            for tap, dst, src in ((0, (s0 + 1, e0), (s0, e0 - 1)),
                                                  (2, (s0, e0 - 1), (s0 + 1, e0))):
                                link(dve.scalar_tensor_tensor(
                                    out=convT[:, c, dst[0]:dst[1]], in0=uT[:, c, src[0]:src[1]],
                                    scalar=colv[:, 3 + 4 * tap + c:4 + 4 * tap + c],
                                    in1=convT[:, c, dst[0]:dst[1]], op0=ALU.mult, op1=ALU.add))
                            s0 = e0
                if b == CONV_B:
                    dve.wait_ge(a_lam, 1)
                    link(dve.tensor_tensor(lam[:, 2:3], lam[:, 1:2], lam[:, 0:1], ALU.subtract))
                    link(dve.tensor_scalar(lam[:, 2:3], lam[:, 2:3], LAMBDA_INIT, None, ALU.subtract))

            for w in range(2, NI + 3):
                if w < NI:
                    scores(w)
                if w <= NI:
                    combine(w - 1)
                if w in LATE_UNITS:
                    split_lo(LATE_UNITS[w])
                if NI <= w < NI + 2:
                    conv_lo(w - NI)

            dve.wait_ge(a_os, 1)
            link(dve.reciprocal(o_ssq[:], o_ssq[:]))
            ors = o_ssq[:].rearrange("p (h i) -> p i h", h=HEADS)

            def o_norm(i):
                ot = o_tok[:, i].rearrange("p (h d) -> p h d", h=HEADS)
                dve.tensor_tensor(ot, ot, ors[:, i].unsqueeze(2).broadcast_to([P, HEADS, VD]),
                                  ALU.mult).then_inc(d_on, 1)

            def mix_lo(i):
                dve.wait_ge(a_mix, i + 1)
                for_lo = mixA[1][:, :, tk(i)]
                b4 = bank[(7, 0)[i % 2]]
                dve.scalar_tensor_tensor(out=for_lo, in0=b4[:].rearrange("p (k t) -> p k t", k=4),
                                         scalar=gs[:], in1=f(mixA[0][:, :, tk(i)]),
                                         op0=ALU.mult, op1=ALU.subtract).then_inc(d_mix, 1)

            def x2_sum(i):
                if i == PROMPT_TILES - 1:
                    dve.wait_ge(d_mixc, TILES)
                dve.wait_ge(xr_ld[i % 2], 16 * (i // 2 + 1))
                for half in range(2):
                    c = slice(half * N, (half + 1) * N)
                    dve.wait_ge(pe_wo, 2 * i + half + 1)
                    dve.tensor_tensor(x2[i][:, c], bank[3 + 2 * (i % 2) + half][:], xr[i % 2][:, c],
                                      ALU.add).then_inc(d_x2, 1)

            o_norm(0)
            for i in range(TILES):
                if i + 1 < TILES:
                    o_norm(i + 1)
                mix_lo(i)
                if i >= 2:
                    conv_lo(i)
                if i == 3:
                    x2_sum(0)

            for i in range(TILES):
                if i == TILES - 1:
                    for u in range(PLE0, MOE0):
                        split_lo(u)
                if i == 0:
                    dve.wait_ge(gain_ld, 32)
                else:
                    x2_sum(i)
                dve.wait_ge(a_x2, 2 * i + 2)
                link(dve.reciprocal(x2_ssq[:, i:i + 1], x2_ssq[:, i:i + 1]))
                for half in range(2):
                    c = slice(half * N, (half + 1) * N)
                    dve.scalar_tensor_tensor(out=h2[i][:, c], in0=x2[i][:, c],
                                             scalar=x2_ssq[:, i:i + 1], in1=gain[:, c],
                                             op0=ALU.mult, op1=ALU.mult).then_inc(d_h2, 1)
            dve.wait_ge(a_p, 1)
            dve.tensor_tensor(pTs[1][:], p_raw[:], f(pTs[0][:]), ALU.subtract).then_inc(d_p, 1)

            def bc(ap, shape):
                return ap.broadcast_to([P, *shape])

            def first_max(out, score, vals, top):
                n4 = [TILES, 4]
                link(dve.tensor_tensor(score[:], vals, bc(top[:].unsqueeze(2), n4), ALU.is_equal))
                link(dve.tensor_tensor(score[:], score[:], bc(cst[:, C_DESC:C_DESC + 4].unsqueeze(1), n4),
                                       ALU.mult))
                link(dve.reduce_max(r_gs[:], score[:], AX_X))
                link(dve.tensor_tensor(out[:], score[:], bc(r_gs[:].unsqueeze(2), n4), ALU.is_equal))

            dve.wait_ge(pe_r, TILES)
            link(dve.tensor_tensor(r_lg[:], bank[7][:, 0:TILES * ROUTES].rearrange(
                "p (i r) -> p i r", i=TILES), bc(bias_row[:].unsqueeze(1), [TILES, ROUTES]), ALU.add))
            lg, le = r_lg[:, :, 0:G], r_lg[:, :, G:ROUTES]
            link(dve.reduce_max(r_gm[:], lg, AX_X))
            dve.tensor_tensor(r_ge[:], lg, bc(r_gm[:].unsqueeze(2), [TILES, G]),
                              ALU.subtract).then_inc(d_lg, 1)
            first_max(r_oh, r_sc, lg, r_gm)
            link(dve.tensor_tensor(
                r_O[0][:], le.rearrange("p i (g e) -> p i g e", g=G),
                bc(r_oh[:].unsqueeze(3), [TILES, G, EPG]), ALU.mult))
            link(dve.reduce_sum(r_sel[:], r_O[0][:].rearrange("p i g e -> p i e g"), AX_X))
            link(dve.reduce_max(r_m1[:], r_sel[:], AX_X))
            first_max(r_o1, r_sc, r_sel[:], r_m1)
            link(dve.scalar_tensor_tensor(out=r_sel[:], in0=r_o1[:], scalar=-1.0e30, in1=r_sel[:],
                                          op0=ALU.mult, op1=ALU.add))
            link(dve.reduce_max(r_m2[:], r_sel[:], AX_X))
            dve.tensor_tensor(r_e2[:], r_m2[:], r_m1[:], ALU.subtract).then_inc(d_lg, 1)
            first_max(r_o2, r_sc, r_sel[:], r_m2)
            for O, pick in zip(r_O, (r_o1, r_o2)):
                link(dve.tensor_tensor(O[:], bc(r_oh[:].unsqueeze(3), [TILES, G, EPG]),
                                       bc(pick[:].unsqueeze(2), [TILES, G, EPG]), ALU.mult))
            flat = [O[:].rearrange("p i g e -> p i (g e)") for O in r_O]
            link(dve.tensor_tensor(r_M[:, 0:TILES], flat[0], flat[1], ALU.add))
            link(dve.memset(r_C[:, 0], 0.0))
            for i in range(1, TILES):
                link(dve.tensor_tensor(r_C[:, i], r_C[:, i - 1], r_M[:, i - 1], ALU.add))
            dve.tensor_tensor(r_M[:, TILES], r_C[:, TILES - 1], r_M[:, TILES - 1],
                              ALU.add).then_inc(d_m, 1)
            dve.wait_ge(a_g, 1)
            link(dve.reduce_sum(r_gs[:], r_ge[:], AX_X))
            dve.wait_ge(a_e2, 1)
            link(dve.scalar_tensor_tensor(out=wgt[:, 0:TILES], in0=r_e2[:], scalar=1.0, in1=r_gs[:],
                                          op0=ALU.add, op1=ALU.mult))
            link(dve.reciprocal(wgt[:, 0:TILES], wgt[:, 0:TILES]))
            link(dve.tensor_tensor(wgt[:, TILES:2 * TILES], wgt[:, 0:TILES], r_e2[:], ALU.mult))
            dve.wait_ge(pe_rk, 1)
            link(dve.tensor_copy(r_cnt[:], bank[0][:, TILES * E:(TILES + 1) * E]))
            link(dve.tensor_tensor(r_ov[:], bc(r_cnt[:].unsqueeze(2), [E, 6]),
                                   bc(cst[:, C_THR:C_THR + 6].unsqueeze(1), [E, 6]), ALU.is_gt))
            link(dve.reduce_sum(r_b[:], r_ov[:], AX_X))
            link(dve.tensor_tensor_scan(r_inc[:], cst[:, C_ONE:C_ONE + E], r_b[:], 0.0, ALU.mult, ALU.add))
            link(dve.tensor_tensor(r_base[:], r_inc[:], r_b[:], ALU.subtract))
            link(dve.scalar_tensor_tensor(out=r_base[:], in0=r_base[:], scalar=float(P),
                                          in1=cst[:, C_K15:C_K15 + E], op0=ALU.mult, op1=ALU.add))
            te = [TILES, E]
            rank = bank[0][:, 0:TILES * E].rearrange("p (i e) -> p i e", i=TILES)
            link(dve.tensor_scalar(r_big[:], rank, float(P), None, ALU.is_ge))
            link(dve.tensor_tensor(r_big[:], r_big[:], bc(r_base[:].unsqueeze(1), te), ALU.mult))
            link(dve.tensor_tensor(r_slot[:], rank, r_big[:], ALU.add))
            link(dve.tensor_tensor(r_slot[:], r_slot[:], bc(cst[:, C_E128:C_E128 + E].unsqueeze(1), te),
                                   ALU.add))
            for j in range(2):
                link(dve.tensor_tensor(r_t[:], r_slot[:], flat[j], ALU.mult))
                link(dve.reduce_sum(r_sl[:, j * TILES:(j + 1) * TILES], r_t[:], AX_X))
            n2 = 2 * TILES
            dve.wait_ge(late_ld, 16)
            dve.wait_ge(h_st, 16 * TILES)
            link(dve.tensor_tensor(ge_sl[:], bc(r_sl[:].unsqueeze(2), [n2, MOE_TILES + 1]),
                                   bc(cl[:, L_SLOT:L_TOK].unsqueeze(1), [n2, MOE_TILES + 1]), ALU.is_ge))
            link(dve.reduce_sum(r_tl[:], ge_sl[:, :, 1:MOE_TILES + 1], AX_X))
            link(dve.scalar_tensor_tensor(out=r_rk[:], in0=r_tl[:], scalar=-float(P), in1=r_sl[:],
                                          op0=ALU.mult, op1=ALU.add))
            link(dve.tensor_tensor(tile_hot[:], ge_sl[:, :, 0:MOE_TILES], ge_sl[:, :, 1:MOE_TILES + 1],
                                   ALU.subtract))
            link(dve.tensor_tensor(tile_hot[:], tile_hot[:],
                                   bc(cl[:, L_TOK:L_N].unsqueeze(2), [n2, MOE_TILES]), ALU.mult))
            for j in range(2):
                c = slice(j * TILES, (j + 1) * TILES)
                dve.tensor_tensor(rank_hot[:, c], bc(cl[:, L_IOTA:L_IOTA + P].unsqueeze(1), [TILES, P]),
                                  bc(r_rk[:, c].unsqueeze(2), [TILES, P]), ALU.is_equal).then_inc(d_hot, 1)
            link(dve.tensor_tensor(r_et[:], bc(r_inc[:].unsqueeze(1), [OVER_TILES, E]),
                                   bc(cst[:, C_T:C_T + OVER_TILES].unsqueeze(2), [OVER_TILES, E]),
                                   ALU.is_le))
            link(dve.reduce_sum(r_ef[:, 0:OVER_TILES], r_et[:], AX_X))
            link(dve.tensor_scalar(r_ef[:, 0:OVER_TILES], r_ef[:, 0:OVER_TILES], float(E - 1), None,
                                   ALU.min))
            link(dve.tensor_scalar(r_ef[:, OVER_TILES:OVER_TILES + 1], r_inc[:, E - 1:E], float(E - 2),
                                   None, ALU.add))
            link(dve.tensor_copy(etab[:, 0:E], cst[:, C_T:C_T + E]))
            link(dve.tensor_copy(etab[:, E:MOE_TILES], r_ef[:, 0:OVER_TILES]))
            dve.tensor_copy(last_tile[:], r_ef[:, OVER_TILES:OVER_TILES + 1]).then_inc(d_route, 1)

            dve.wait_ge(pe_tab, 1)
            dve.tensor_copy(src_u[:], bank[7][:, 0:MOE_TILES]).then_inc(d_tab, 1)
            dve.tensor_copy(slot_u[:], r_sl[:]).then_inc(d_tab, 1)
            for j in range(4):
                split_lo(MOE0 + j)
            dve.wait_ge(ach, 2 * TILES)
            link(dve.reciprocal(e_ssq[:], e_ssq[:]))

            dve.wait_ge(d_route, 1)
            m = dve.value_load(last_tile[0:1, 0:1], min_val=E - 2, max_val=MOE_TILES - 2)

            def xT_lo(t, half):
                dve.wait_ge(a_xt, t * 2 + (half + 1))
                dve.tensor_tensor(xgT[1][:, 4 * half:4 * half + 4],
                                  bank[1 + half][:].rearrange("p (k t) -> p k t", k=4),
                                  f(xgT[0][:, 4 * half:4 * half + 4]), ALU.subtract).then_inc(d_xt, 1)

            def act_mul(t):
                dve.wait_ge(a_si, t + 1)
                dve.tensor_tensor(act_t[:], bank[0][:, DE:2 * DE], sg[:], ALU.mult).then_inc(d_act, 1)

            def actT_lo(t):
                dve.wait_ge(a_aT2, t + 1)
                dve.tensor_tensor(actT[1][:], bank[3][:, 0:DE].rearrange("p (k t) -> p k t", k=2),
                                  f(actT[0][:]), ALU.subtract).then_inc(d_aT2, 1)

            def y_right(t):
                dve.wait_ge(pe_y, t * 2 + 2)
                dve.wait_ge(y_st[1], t * 16 + 16)
                dve.tensor_copy(yb[:, 1], bank[5][:]).then_inc(d_y, 1)

            def moe_lo(u, t, slot):
                dve.wait_ge(hi_done, t * 6 + (u + 1))
                dve.tensor_tensor(W[:, slot, 1], raw(u)[0], f(W[:, slot, 0]),
                                  ALU.subtract).then_inc(lo_done, 1)

            dve.sem_inc(d_y, 1)
            xT_lo(0, 0)
            xT_lo(0, 1)
            for j in range(3):
                moe_lo(UP1 + j, 0, 2 + j)
            act_mul(0)
            xT_lo(1, 0)
            xT_lo(1, 1)
            moe_lo(UP1 + 3, 0, 5)
            for j in range(2):
                moe_lo(DOWN0 + j, 0, 6 + j)
            with dve.Fori(0, m) as t:
                moe_lo(UP1 + 6, t, 2)
                actT_lo(t)
                moe_lo(UP1 + 7, t, 3)
                moe_lo(UP1 + 8, t, 4)
                act_mul(t + 1)
                xT_lo(t + 2, 0)
                xT_lo(t + 2, 1)
                moe_lo(UP1 + 9, t, 5)
                y_right(t)
                for j in range(2):
                    moe_lo(DOWN0 + 6 + j, t, 6 + j)
            actT_lo(m)
            act_mul(m + 1)
            for j in range(2):
                moe_lo(DOWN_LAST + j, m, j)
            y_right(m)
            actT_lo(m + 1)
            moe_lo(GATE0, m, 2)
            y_right(m + 1)
            for g in range(1, FIN_UNITS):
                moe_lo(GATE0 + g, m, (g + 2) % WS)

            def x3(i):
                dve.wait_ge(pk_ld[i % 2], 32 * (i // 2 + 1))
                for half in range(2):
                    h_ = slice(half * N, (half + 1) * N)
                    for j, buf in ((0, ga), (1, gb)):
                        c = j * TILES + i
                        ins = dve.scalar_tensor_tensor(out=x2[i][:, h_], in0=buf[i % 2][:, h_],
                                                       scalar=wgt[:, c:c + 1], in1=x2[i][:, h_],
                                                       op0=ALU.mult, op1=ALU.add)
                        if j == 0:
                            link(ins)
                        else:
                            ins.then_inc(d_x3, 1)

            def x3T_lo(i):
                for half in range(2):
                    dve.wait_ge(a_x3, 2 * i + half + 1)
                    dve.tensor_tensor(x3T[i % 2][1][:, 4 * half:4 * half + 4],
                                      bank[6 + half][:].rearrange("p (k t) -> p k t", k=4),
                                      f(x3T[i % 2][0][:, 4 * half:4 * half + 4]),
                                      ALU.subtract).then_inc(d_x3t, 1)

            dve.wait_ge(g_ple, TILES)
            x3(0)
            x3T_lo(0)
            for i in range(TILES):
                if i + 1 < TILES:
                    x3(i + 1)
                    x3T_lo(i + 1)
                for half in range(2):
                    c = slice(half * N, (half + 1) * N)
                    dve.wait_ge(a_g2, 2 * i + half + 1)
                    if i >= 1:
                        dve.wait_ge(o_st[half], 16 * i)
                    link(dve.scalar_tensor_tensor(out=outb[:, c], in0=sig[:, c],
                                                  scalar=e_ssq[:, i:i + 1], in1=ple[i][:, c],
                                                  op0=ALU.mult, op1=ALU.mult))
                    dve.tensor_tensor(outb[:, c], outb[:, c], x2[i][:, c],
                                      ALU.add).then_inc(d_out, 1)

        @block.tensor
        def _(pe):
            def turn(out, src, k, inc, first=0):
                for q in range(k):
                    ins = pe.transpose(out[:, q * P:(q + 1) * P], src[:, (first + q) * P:(first + q + 1) * P],
                                       ident)
                ins.then_inc(inc, 1)

            def turn_back(out, src, inc):
                for q in range(4):
                    ins = pe.matmul(out[:, q * P:(q + 1) * P], src[:, q * P:(q + 1) * P],
                                    cst[:, C_J:C_J + P], start=True, stop=True)
                ins.then_inc(inc, 1)

            def t_bank(m):
                if m >= 4:
                    pe.wait_ge(t_free[m % 4], m // 4)
                return bank[3 + m % 4]

            def turn_h(i):
                pe.wait_ge(d_x, 2 * i + 2)
                for half in range(2):
                    turn(t_bank(2 * i + half), xt[i], 4, pe_t, 4 * half)

            def scores(w):
                h, i = ITEMS[w]
                k0, nk = keys(i)
                pe.wait_ge(p_pad, 2 * w + 2)
                if w >= 2:
                    pe.wait_ge(d_s, 2 * (w - 1))
                for m in range(2):
                    pe.matmul(bank[3 + 2 * (w % 2) + m][:, 0:nk], pad[w % 2][:, m], kT[:, h, k0:k0 + nk],
                              start=True, stop=True).then_inc(pe_s, 1)

            def turn_a(w):
                nk = keys(ITEMS[w][1])[1]
                pe.wait_ge(d_a, w + 1)
                if w >= 2:
                    pe.wait_ge(a_at, w - 1)
                turn(bank[(7, 0)[w % 2]], s_sb[w % 2][0], nk // P, pe_at)

            def pv(w):
                h, i = ITEMS[w]
                k0, nk = keys(i)
                pe.wait_ge(a_at, w + 1)
                if w >= 2:
                    pe.wait_ge(a_o, 2 * (w - 1))
                for q in range(nk // P):
                    ins = pe.matmul(bank[1 + w % 2][:, 0:VD], aT[w % 2][:, q * P:(q + 1) * P],
                                    v[:, k0 // P + q, h * VD:(h + 1) * VD],
                                    start=(q == 0), stop=(q == nk // P - 1))
                ins.then_inc(pe_o, 1)

            def out_part(i, half, ks, src):
                for k in ks:
                    u = OUT0 + 4 * half + k // 2
                    if i == 0 and k % 2 == 0:
                        pe.wait_ge(lo_done, u + 1)
                    w = W[:, u % WS]
                    ins = three(bank[3 + 2 * (i % 2) + half][:], src[0][:, k % 4, tk(i)],
                                src[1][:, k % 4, tk(i)], w[:, 0, k % 2], w[:, 1, k % 2],
                                k == 0, k == KD - 1)
                    if k == KD - 1:
                        ins.then_inc(pe_wo, 1)
                    elif i == TILES - 1 and k % 2:
                        ins.then_inc(w_used, 1)

            def conv_part(i, half):
                pe.wait_ge(d_mixc, i + 1)
                if i >= 2:
                    pe.wait_ge(d_x2, 2 * (i - 2) + half + 1)
                out_part(i, half, range(4), mixC)

            def att_part(i, half):
                pe.wait_ge(d_mix, i + 1)
                out_part(i, half, range(4, KD), mixA)

            pe.wait_ge(id_ld, 16)
            turn_h(0)
            turn_h(1)
            for b in range(6):
                for i in range(TILES):
                    n = TILES * b + i
                    if b == 0:
                        t_ready(pe, 2 * i)
                        t_ready(pe, 2 * i + 1)
                    if n >= 3:
                        pe.wait_ge(acc_free[n % 3], n // 3)
                    for k in range(KD):
                        u = 4 * b + k // 2
                        if i == 0 and k % 2 == 0:
                            pe.wait_ge(lo_done, u + 1)
                        w = W[:, u % WS]
                        ins = three(bank[n % 3][:], hT[:, 0, k, tk(i)], hT[:, 1, k, tk(i)],
                                    w[:, 0, k % 2], w[:, 1, k % 2], k == 0, k == KD - 1)
                        if k == KD - 1:
                            ins.then_inc(pe_acc, 1)
                        elif i == TILES - 1 and k % 2:
                            ins.then_inc(w_used, 1)
                    if b == 0 and i + 2 < TILES:
                        turn_h(i + 2)
                    pb, pi = divmod(n - 1, TILES)
                    if n >= 1 and pb in TJ:
                        m = TJ[pb] + pi
                        src = u_tok[:, pi] if pb == X_B else tok_tmp[pi % 2]
                        out = t_bank(m)
                        pe.wait_ge(acc_free[(n - 1) % 3], (n - 1) // 3 + 1)
                        if pb == Q_B:
                            turn_back(out, src, pe_t)
                        else:
                            turn(out, src, 4, pe_t)
                    if b == V_B and i in (2, 4):
                        if i == 2:
                            for m in range(32, 36):
                                t_ready(pe, m)
                        scores(i // 2 - 1)
                if b == CONV_B:
                    pe.wait_ge(c_ld, 16 * 6)
                    for half in range(2):
                        if half:
                            pe.wait_ge(a_b, half)
                        pe.matmul(bank[7][0:MAPS], relb[0:BUCKETS, :], hot_sb[:, half * N:(half + 1) * N],
                                  start=True, stop=True).then_inc(pe_b, 1)

            for n in range(33, 36):
                pe.wait_ge(acc_free[n % 3], n // 3 + 1)
            for w in range(2, NI + 3):
                if w < NI:
                    scores(w)
                if w < NI + 2:
                    turn_a(w - 2)
                if w >= 3:
                    pv(w - 3)
                if w == NI:
                    pe.wait_ge(d_s, 2 * NI)
                if w >= NI:
                    conv_part(*((0, 0), (0, 1), (1, 0))[w - NI])
            conv_part(1, 1)
            def turn_o(i):
                pe.wait_ge(d_on, i + 1)
                if i >= 2:
                    pe.wait_ge(d_mix, i - 1)
                turn_back(bank[(7, 0)[i % 2]], o_tok[:, i], pe_ot)

            def turn_h2(i):
                for half in range(2):
                    pe.wait_ge(d_h2, 2 * i + half + 1)
                    if i >= 1:
                        pe.wait_ge(a_h2, 2 * (i - 1) + half + 1)
                    turn(bank[1 + half], h2[i], 4, pe_h2, 4 * half)

            def router(i):
                pe.wait_ge(a_h2, 2 * i + 2)
                for k in range(KD):
                    ins = pe.matmul(bank[7][:, i * ROUTES:(i + 1) * ROUTES], h2T[:, k], wr[:, k],
                                    start=(k == 0), stop=(k == KD - 1))
                ins.then_inc(pe_r, 1)

            for i in range(3):
                turn_o(i)
            for i in range(TILES):
                if i >= 2:
                    conv_part(i, 0)
                if i == 2:
                    pe.wait_ge(d_mix, TILES)
                if i >= 2:
                    router(i - 2)
                att_part(i, 0)
                if i < 2:
                    turn_o(3 + 2 * i)
                if i >= 2:
                    conv_part(i, 1)
                att_part(i, 1)
                if i == 0:
                    turn_o(4)
                if i >= 1:
                    turn_h2(i - 1)
            router(TILES - 2)
            turn_h2(TILES - 1)

            def ple_proj(i):
                for half in range(2):
                    u = PLE0 + half
                    if i == 0:
                        pe.wait_ge(lo_done, u + 1)
                    if i < 2:
                        pe.wait_ge(d_x2, 2 * (TILES - 2 + i) + half + 1)
                    else:
                        pe.wait_ge(a_ple, 3 * (i - 2) + half + 1)
                    w = W[:, u % WS]
                    for k in range(2):
                        ins = three(bank[3 + 2 * (i % 2) + half][:], pTs[0][:, k, tk(i)],
                                    pTs[1][:, k, tk(i)], w[:, 0, k], w[:, 1, k], k == 0, k == 1)
                    ins.then_inc(pe_ple, 1)

            router(TILES - 1)
            pe.wait_ge(d_p, 1)
            ple_proj(0)
            ple_proj(1)
            pe.wait_ge(d_m, 1)
            rk = bank[0]
            pe.matmul(rk[:, 0:TILES * E], cst[:, C_U:C_U + P], r_M[:, 0:TILES].rearrange("p i e -> p (i e)"),
                      start=True, stop=False)
            pe.matmul(rk[:, 0:TILES * E], cst[:, C_ONE:C_ONE + P], r_C[:].rearrange("p i e -> p (i e)"),
                      start=False, stop=True)
            pe.matmul(rk[:, TILES * E:(TILES + 1) * E], cst[:, C_ONE:C_ONE + P], r_M[:, TILES],
                      start=True, stop=True).then_inc(pe_rk, 1)
            for i in range(2, TILES - 1):
                ple_proj(i)
            for j in range(2):
                pe.wait_ge(d_hot, j + 1)
                for c in range(j * TILES, (j + 1) * TILES):
                    ins = pe.matmul(bank[7][:, 0:MOE_TILES], rank_hot[:, c], tile_hot[:, c],
                                    start=(c == 0), stop=(c == 2 * TILES - 1))
            ins.then_inc(pe_tab, 1)
            ple_proj(TILES - 1)

            pe.wait_ge(d_route, 1)
            m = pe.value_load(last_tile[0:1, 0:1], min_val=E - 2, max_val=MOE_TILES - 2)

            def turn_x(t):
                pe.wait_ge(xg_ld, t * 16 + 16)
                for half in range(2):
                    turn(bank[1 + half], xg, 4, pe_xt, 4 * half)

            def gate_up(t, ks, u0, t0):
                for k in ks:
                    if k % 2 == 0:
                        pe.wait_ge(lo_done, t0 * 6 + (u0 + k // 2 + 1))
                    w = W[:, 2 + k // 2]
                    ins = three(bank[0][:], xgT[0][:, k], xgT[1][:, k], w[:, 0, k % 2], w[:, 1, k % 2],
                                k == 0, k == KD - 1)
                    if k == KD - 1:
                        ins.then_inc(pe_gu, 1)
                    elif k % 2:
                        ins.then_inc(w_used, 1)

            def next_up(t):
                pe.wait_ge(d_xt, t * 2 + 4)
                pe.wait_ge(d_act, t + 1)
                gate_up(t + 1, range(4), UP1, t)
                turn(bank[3], act_t, 2, pe_aT2)
                gate_up(t + 1, range(4, KD), UP1, t)

            def down(t, u0, t0, slot=6):
                pe.wait_ge(d_aT2, t + 1)
                for half, free in ((0, a_y), (1, d_y)):
                    pe.wait_ge(free, t + 1)
                    pe.wait_ge(lo_done, t0 * 6 + (u0 + half + 1))
                    w = W[:, slot + half]
                    for k in range(2):
                        ins = three(bank[4 + half][:], actT[0][:, k], actT[1][:, k], w[:, 0, k],
                                    w[:, 1, k], k == 0, k == 1)
                    ins.then_inc(pe_y, 1)

            turn_x(0)
            pe.wait_ge(d_xt, 2)
            gate_up(0, range(KD), MOE0, 0)
            pe.wait_ge(a_ple, 3 * TILES)
            turn_x(1)
            with pe.Fori(0, m) as t:
                next_up(t)
                turn_x(t + 2)
                down(t, DOWN0, t)
            next_up(m)
            down(m, DOWN0, m)
            pe.wait_ge(d_act, m + 2)
            turn(bank[3], act_t, 2, pe_aT2)
            down(m + 1, DOWN_LAST, m, 0)

            def turn_x3(i):
                for half in range(2):
                    pe.wait_ge(d_x3, 2 * i + half + 1)
                    if i >= 1:
                        pe.wait_ge(d_x3t, 2 * (i - 1) + half + 1)
                    turn(bank[6 + half], x2[i], 4, pe_x3, 4 * half)

            def gate(i, half):
                if half == 0:
                    pe.wait_ge(d_x3t, 2 * i + 2)
                if i >= 2:
                    pe.wait_ge(a_g2, 2 * (i - 2) + half + 1)
                for k in range(KD):
                    g = 4 * half + k // 2
                    if i == 0 and k % 2 == 0:
                        pe.wait_ge(lo_done, m * 6 + (GATE0 + g + 1))
                    w = W[:, (g + 2) % WS]
                    ins = three(bank[2 * (i % 2) + half][:], x3T[i % 2][0][:, k], x3T[i % 2][1][:, k],
                                w[:, 0, k % 2], w[:, 1, k % 2], k == 0, k == KD - 1)
                ins.then_inc(pe_g, 1)

            turn_x3(0)
            for i in range(TILES):
                gate(i, 0)
                if i + 1 < TILES:
                    turn_x3(i + 1)
                gate(i, 1)


def units(w):
    k, n = w.shape
    return np.ascontiguousarray(
        w.reshape(k // 256, 2, P, n // N, N).transpose(3, 0, 2, 1, 4).reshape(-1, P, 2, N))


def kernel(**inputs):
    import concourse.bacc as _bacc
    from concourse.bass_utils import run_bass_kernel_spmd as _run

    a = {k: np.asarray(v) for k, v in inputs.items()}
    x = np.concatenate([a["x_prompt"][0], a["x_sample"][0]])
    p = np.concatenate([a["p_prompt"][0, 0], a["p_sample"][0, 0]])
    w_in = a["w_in"][0]
    order = [4, 5, 3, 0, 1, 2]
    w_in = np.concatenate([w_in[:, N * b:N * (b + 1)] for b in order], axis=1)
    gu = a["w_gate_up"][0].reshape(E, 4, 2, P, N).transpose(0, 1, 3, 2, 4)
    dn = a["w_down"][0].reshape(E, 2, P, 2, N).transpose(0, 3, 2, 1, 4)
    conv = a["conv_w"][0].reshape(3, 4, P).transpose(2, 0, 1).reshape(P, 12)
    cst, hot, late = constants()
    data = {
        "x": x,
        "pT": p.T.reshape(2, P, TOK).transpose(1, 0, 2),
        "w_in": units(w_in),
        "w_out": units(np.roll(a["w_out"][0], D_ATT, axis=0)),
        "w_ple": units(a["w_ple_proj"][0]),
        "w_moe": np.concatenate([gu, dn], axis=1),
        "w_gate": units(a["w_ple_gate"][0]),
        "w_route": np.concatenate([a["w_group"][0], a["w_erouter"][0]], axis=1).reshape(
            KD, P, ROUTES).transpose(1, 0, 2),
        "gains": np.stack([np.broadcast_to(a[k][0], (P, D)) for k in ("norm_mix", "norm_ffn", "ple_norm")]),
        "cols": np.concatenate([np.concatenate([a["q_norm"][0]] * 2)[:, None],
                                np.concatenate([a["k_norm"][0]] * 2)[:, None],
                                a["attn_sub_norm"][0][:, None], conv], axis=1),
        "rows": np.broadcast_to(np.concatenate([
            a["lambda_q1"][0], a["lambda_k1"][0], a["lambda_q2"][0], a["lambda_k2"][0],
            a["b_group"][0], a["b_erouter"][0]]), (P, 4 * HD + ROUTES)),
        "rel_bias": a["rel_bias"],
        "consts": cst,
        "hot": hot,
        "late": late,
    }
    nc = _bacc.Bacc("TRN2", target_bir_lowering=False, num_devices=1)
    arrays, args = {}, {}
    for name, arr in data.items():
        arr = np.ascontiguousarray(arr)
        arrays[f"in_{name}"] = arr
        args[name] = nc.dram_tensor(f"in_{name}", arr.shape, mybir.dt.from_np(arr.dtype),
                                    kind="ExternalInput").ap()
    for name, s in (("y_prompt", SEQS[0]), ("y_sample", SEQS[1])):
        args[name] = nc.dram_tensor(f"out_{name}", (s, D), F32, kind="ExternalOutput").ap()
    build(nc, **args)
    r = _run(nc, [arrays], core_ids=[0])
    return tuple(np.asarray(r.results[0][f"out_{n}"]).reshape(1, s, D)
                 for n, s in (("y_prompt", SEQS[0]), ("y_sample", SEQS[1])))
```
